# Optimizing a Trainium2 kernel written in Bass

```python
import math
import jax, jax.numpy as jnp
from jax import lax
import numpy as np

D_MODEL = 1024
BATCH = 1
SEQ = 512
DEPTH = 1

CTX_LEN = 256
GRID_W = 64

GDN_HEADS = 4
GDN_HEAD_DIM = 128
GDN_WIDTH = GDN_HEADS * GDN_HEAD_DIM
CONV_W = 5
CHUNK = 64
ROPE_BASE = 10000.0

NA_HEADS = 8
NA_HEAD_DIM = 64
NA_WIDTH = NA_HEADS * NA_HEAD_DIM
NA_ROWS = 8
NA_COLS = 16

MIX_WIDTH = GDN_WIDTH + NA_WIDTH
IN_COLS = 4 * GDN_WIDTH + 4 * GDN_HEADS + 3 * NA_WIDTH

N_EXPERTS = 16
CAPACITY_FACTOR = 2
D_EXPERT = 1024

EPS = 1e-6


def rms_norm(x, w):
    xf = x.astype(jnp.float32)
    y = xf * lax.rsqrt(jnp.mean(xf * xf, axis=-1, keepdims=True) + EPS)
    return y.astype(x.dtype) * w

def l2_normalize(t):
    tf = t.astype(jnp.float32)
    return (tf * lax.rsqrt(jnp.sum(tf * tf, axis=-1, keepdims=True) + EPS)).astype(t.dtype)

def modulate(h, shift, scale):
    return h * (1.0 + scale) + shift

def depthwise_conv(x, w):
    C = x.shape[-1]
    return lax.conv_general_dilated(
        x, w[:, None, :].astype(x.dtype), window_strides=(1,),
        padding=((CONV_W // 2, CONV_W // 2),),
        dimension_numbers=('NWC', 'WIO', 'NWC'), feature_group_count=C)

def axial_rope(x):
    T, D = x.shape[1], x.shape[-1]
    half = D // 2
    pairs = half // 2
    t = jnp.arange(T)
    inv_freq = ROPE_BASE ** (-jnp.arange(pairs, dtype=jnp.float32) / pairs)

    def rot(xa, pos):
        ang = pos.astype(jnp.float32)[:, None] * inv_freq[None, :]
        cos = jnp.cos(ang)[None, :, None, :].astype(x.dtype)
        sin = jnp.sin(ang)[None, :, None, :].astype(x.dtype)
        x1, x2 = xa[..., :pairs], xa[..., pairs:]
        return jnp.concatenate([x1 * cos - x2 * sin, x2 * cos + x1 * sin], axis=-1)

    return jnp.concatenate([rot(x[..., :half], t // GRID_W), rot(x[..., half:], t % GRID_W)], axis=-1)

def gdn_inputs(p_qkv, p_a, p_b, conv_w, a_log, dt_bias, rotary):
    B, T, _ = p_qkv.shape
    qkv = jax.nn.silu(depthwise_conv(p_qkv, conv_w))
    q, k, v = jnp.split(qkv, 3, axis=-1)
    heads = lambda t: t.reshape(B, T, GDN_HEADS, GDN_HEAD_DIM)
    q, k, v = l2_normalize(heads(q)), l2_normalize(heads(k)), heads(v)
    if rotary:
        q, k = axial_rope(q), axial_rope(k)
    a = p_a.astype(jnp.float32).reshape(B, T, 2, GDN_HEADS)
    b = p_b.astype(jnp.float32).reshape(B, T, 2, GDN_HEADS)
    g = -jnp.exp(a_log.astype(jnp.float32)) * jax.nn.softplus(a + dt_bias.astype(jnp.float32))
    beta = jax.nn.sigmoid(b)
    return q, k, v, g, beta

def chunk_gated_delta(q, k, v, g, beta, s0):
    B, H, T, dk = k.shape
    dv = v.shape[-1]
    n = T // CHUNK
    q = q * (dk ** -0.5)
    q, k, v = [t.reshape(B, H, n, CHUNK, t.shape[-1]) for t in (q, k, v)]
    g = g.reshape(B, H, n, CHUNK)
    beta = beta.reshape(B, H, n, CHUNK)
    gcum = jnp.cumsum(g, axis=-1)
    incl = jnp.tril(jnp.ones((CHUNK, CHUNK), dtype=bool))
    strict = jnp.tril(jnp.ones((CHUNK, CHUNK), dtype=bool), -1)
    decay = jnp.exp(jnp.where(incl, gcum[..., :, None] - gcum[..., None, :], -jnp.inf))
    kb = k * beta[..., None]
    lower = jnp.where(strict, jnp.einsum('bhnid,bhnjd->bhnij', kb, k) * decay, 0.0)
    eye = jnp.eye(CHUNK, dtype=jnp.float32)
    tinv = lax.linalg.triangular_solve(eye + lower, jnp.broadcast_to(eye, lower.shape),
                                       left_side=True, lower=True, unit_diagonal=True)
    u = tinv @ (v * beta[..., None])
    w = tinv @ (kb * jnp.exp(gcum)[..., None])
    attn = jnp.where(incl, jnp.einsum('bhnid,bhnjd->bhnij', q, k) * decay, 0.0)
    q_dec = q * jnp.exp(gcum)[..., None]
    k_dec = k * jnp.exp(gcum[..., -1:] - gcum)[..., None]
    g_last = jnp.exp(gcum[..., -1])
    xs = tuple(jnp.moveaxis(t, 2, 0) for t in (q_dec, k_dec, u, w, attn, g_last))

    def step(S, inp):
        qd, kd, ui, wi, ai, gl = inp
        v_new = ui - wi @ S
        o = qd @ S + ai @ v_new
        S = S * gl[..., None, None] + jnp.einsum('bhcd,bhce->bhde', kd, v_new)
        return S, o

    S, o = lax.scan(step, s0, xs)
    return jnp.moveaxis(o, 0, 2).reshape(B, H, T, dv), S

def bidirectional_gated_delta(lat, cin):
    q, k, v, g, beta = lat
    qc, kc, vc, gc, bc = cin
    B = q.shape[0]
    bhtd = lambda t: jnp.swapaxes(t, 1, 2).astype(jnp.float32)
    bht = lambda t, d: jnp.swapaxes(t[:, :, d, :], 1, 2).astype(jnp.float32)
    s0 = jnp.zeros((B, GDN_HEADS, GDN_HEAD_DIM, GDN_HEAD_DIM), jnp.float32)
    outs_l, outs_c = [], []
    for d in range(2):
        order = (lambda t: jnp.flip(t, axis=2)) if d == 1 else (lambda t: t)
        oc, s_ctx = chunk_gated_delta(order(bhtd(qc)), order(bhtd(kc)), order(bhtd(vc)),
                                      order(bht(gc, d)), order(bht(bc, d)), s0)
        ol, _ = chunk_gated_delta(order(bhtd(q)), order(bhtd(k)), order(bhtd(v)),
                                  order(bht(g, d)), order(bht(beta, d)), s_ctx)
        outs_l.append(order(ol))
        outs_c.append(order(oc))
    o_l = jnp.swapaxes(outs_l[0] + outs_l[1], 1, 2).astype(q.dtype)
    o_c = jnp.swapaxes(outs_c[0] + outs_c[1], 1, 2).astype(q.dtype)
    return o_l, o_c

def gated_rms_norm(o, gate, w):
    B, T, H, dv = o.shape
    y = rms_norm(o, w) * jax.nn.silu(gate.reshape(B, T, H, dv))
    return y.reshape(B, T, H * dv)

def neighbourhood_attention(q, k, v, kc, vc, rpb):
    B, T, H, dh = q.shape
    rows = T // GRID_W
    win_rows = min(NA_ROWS, rows)
    grid = lambda t: t.reshape(B, rows, GRID_W, H, dh)
    qg, kg, vg = grid(q * (dh ** -0.5)), grid(k), grid(v)
    col = jnp.arange(GRID_W)
    col_start = jnp.clip(col - NA_COLS // 2, 0, GRID_W - NA_COLS)
    col_in = (col[None, :] >= col_start[:, None]) & (col[None, :] < col_start[:, None] + NA_COLS)
    col_idx = jnp.clip(col[None, :] - col[:, None], -(NA_COLS - 1), NA_COLS - 1) + (NA_COLS - 1)
    rpb_f = rpb.astype(jnp.float32)
    n_lat = win_rows * GRID_W

    def row_block(r):
        start = jnp.clip(r - win_rows // 2, 0, rows - win_rows)
        kr = lax.dynamic_slice_in_dim(kg, start, win_rows, axis=1)
        vr = lax.dynamic_slice_in_dim(vg, start, win_rows, axis=1)
        qr = lax.dynamic_index_in_dim(qg, r, axis=1, keepdims=False)
        row_idx = start + jnp.arange(win_rows) - r + (NA_ROWS - 1)
        bias = rpb_f[:, row_idx][:, :, col_idx].transpose(0, 2, 1, 3)
        s_lat = jnp.einsum('bqhd,brkhd->bhqrk', qr, kr).astype(jnp.float32) + bias[None]
        s_lat = jnp.where(col_in[:, None, :], s_lat, -jnp.inf)
        s_ctx = jnp.einsum('bqhd,bchd->bhqc', qr, kc).astype(jnp.float32)
        s = jnp.concatenate([s_lat.reshape(B, H, GRID_W, n_lat), s_ctx], axis=-1)
        p = jax.nn.softmax(s, axis=-1).astype(q.dtype)
        p_lat = p[..., :n_lat].reshape(B, H, GRID_W, win_rows, GRID_W)
        p_ctx = p[..., n_lat:]
        return (jnp.einsum('bhqrk,brkhd->bqhd', p_lat, vr)
                + jnp.einsum('bhqc,bchd->bqhd', p_ctx, vc))

    out = lax.map(row_block, jnp.arange(rows))
    return jnp.moveaxis(out, 0, 1).reshape(B, T, H * dh)

def context_attention(qc, kc, vc):
    B, Tc, H, dh = qc.shape
    s = jnp.einsum('bqhd,bkhd->bhqk', qc * (dh ** -0.5), kc).astype(jnp.float32)
    p = jax.nn.softmax(s, axis=-1).astype(qc.dtype)
    return jnp.einsum('bhqk,bkhd->bqhd', p, vc).reshape(B, Tc, H * dh)

def token_mixer(h, hc, w_in, conv_qkv, a_log, dt_bias, gdn_norm, na_rpb, w_out, need_ctx):
    B, T, _ = h.shape
    Tc = hc.shape[1]
    cuts = (3 * GDN_WIDTH, 4 * GDN_WIDTH, 4 * GDN_WIDTH + 2 * GDN_HEADS, 4 * GDN_WIDTH + 4 * GDN_HEADS)
    qkv, gate, a, b, na = jnp.split(h @ w_in, cuts, axis=-1)
    qkv_c, gate_c, a_c, b_c, na_c = jnp.split(hc @ w_in, cuts, axis=-1)
    lat = gdn_inputs(qkv, a, b, conv_qkv, a_log, dt_bias, True)
    cin = gdn_inputs(qkv_c, a_c, b_c, conv_qkv, a_log, dt_bias, False)
    o_gdn, o_gdn_c = bidirectional_gated_delta(lat, cin)
    y_gdn = gated_rms_norm(o_gdn, gate, gdn_norm)
    na_heads = lambda t, n: t.reshape(B, n, 3, NA_HEADS, NA_HEAD_DIM)
    nl = na_heads(na, T)
    ncx = na_heads(na_c, Tc)
    y_na = neighbourhood_attention(nl[:, :, 0], nl[:, :, 1], nl[:, :, 2], ncx[:, :, 1], ncx[:, :, 2], na_rpb)
    y = jnp.concatenate([y_gdn, y_na], axis=-1) @ w_out
    if not need_ctx:
        return y, None
    y_c_gdn = gated_rms_norm(o_gdn_c, gate_c, gdn_norm)
    y_c_na = context_attention(ncx[:, :, 0], ncx[:, :, 1], ncx[:, :, 2])
    y_c = jnp.concatenate([y_c_gdn, y_c_na], axis=-1) @ w_out
    return y, y_c

def expert_choice_ffn(h, w_router, w_gate, w_up, w_down):
    B, T, D = h.shape
    cap = CAPACITY_FACTOR * T // N_EXPERTS
    aff = jax.nn.softmax((h @ w_router).astype(jnp.float32), axis=-1)
    gval, idx = lax.top_k(jnp.swapaxes(aff, 1, 2), cap)
    xe = jax.vmap(lambda hb, ib: hb[ib])(h, idx)
    hid = jax.nn.silu(jnp.einsum('becd,edf->becf', xe, w_gate)) * jnp.einsum('becd,edf->becf', xe, w_up)
    ye = jnp.einsum('becf,efd->becd', hid, w_down) * gval[..., None].astype(h.dtype)
    return jax.vmap(lambda yb, ib: jnp.zeros((T, D), yb.dtype).at[ib.reshape(-1)].add(yb.reshape(-1, D)))(ye, idx)

def first_inputs(seed: int = 0) -> dict:
    key = jax.random.key(seed)
    ks = jax.random.split(key, 20)
    f32 = jnp.float32
    nrm = lambda k, shape, s: jax.random.normal(k, shape, f32) * s
    D = D_MODEL
    dt = jnp.exp(jax.random.uniform(ks[11], (DEPTH, 2, GDN_HEADS), f32, math.log(1e-3), math.log(1e-1)))
    return {
        'x': nrm(ks[0], (BATCH, SEQ, D), 1.0),
        'c': nrm(ks[1], (BATCH, D), 1.0),
        'ctx': nrm(ks[2], (BATCH, CTX_LEN, D), 1.0),
        'c_ctx': nrm(ks[3], (D,), 1.0),
        'w_mod': nrm(ks[4], (DEPTH, D, 6 * D), 0.5 * D ** -0.5),
        'b_mod': nrm(ks[5], (DEPTH, 6 * D), 0.02),
        'norm_mix': 1.0 + nrm(ks[6], (DEPTH, D), 0.1),
        'norm_ffn': 1.0 + nrm(ks[7], (DEPTH, D), 0.1),
        'w_in': nrm(ks[8], (DEPTH, D, IN_COLS), D ** -0.5),
        'conv_qkv': nrm(ks[9], (DEPTH, CONV_W, 3 * GDN_WIDTH), CONV_W ** -0.5),
        'a_log': jnp.log(jax.random.uniform(ks[10], (DEPTH, 2, GDN_HEADS), f32, 1.0, 16.0)),
        'dt_bias': dt + jnp.log(-jnp.expm1(-dt)),
        'gdn_norm': 1.0 + nrm(ks[12], (DEPTH, GDN_HEAD_DIM), 0.1),
        'na_rpb': nrm(ks[13], (DEPTH, NA_HEADS, 2 * NA_ROWS - 1, 2 * NA_COLS - 1), 0.2),
        'w_out': nrm(ks[14], (DEPTH, MIX_WIDTH, D), MIX_WIDTH ** -0.5),
        'w_router': nrm(ks[15], (DEPTH, D, N_EXPERTS), D ** -0.5),
        'w_gate': nrm(ks[16], (DEPTH, N_EXPERTS, D, D_EXPERT), D ** -0.5),
        'w_up': nrm(ks[17], (DEPTH, N_EXPERTS, D, D_EXPERT), D ** -0.5),
        'w_down': nrm(ks[18], (DEPTH, N_EXPERTS, D_EXPERT, D), D_EXPERT ** -0.5),
        'final_norm': 1.0 + nrm(ks[19], (D,), 0.1),
    }

def first_block(x, c, ctx, c_ctx, w_mod, b_mod, norm_mix, norm_ffn, w_in, conv_qkv, a_log, dt_bias,
              gdn_norm, na_rpb, w_out, w_router, w_gate, w_up, w_down, final_norm):
    for li in range(DEPTH):
        need_ctx = li + 1 < DEPTH
        mod = jax.nn.silu(c) @ w_mod[li] + b_mod[li]
        mod_c = jax.nn.silu(c_ctx) @ w_mod[li] + b_mod[li]
        sh1, sc1, gt1, sh2, sc2, gt2 = jnp.split(mod[:, None, :], 6, axis=-1)
        sh1c, sc1c, gt1c, sh2c, sc2c, gt2c = jnp.split(mod_c, 6, axis=-1)
        h = modulate(rms_norm(x, norm_mix[li]), sh1, sc1)
        hc = modulate(rms_norm(ctx, norm_mix[li]), sh1c, sc1c)
        y, y_c = token_mixer(h, hc, w_in[li], conv_qkv[li], a_log[li], dt_bias[li], gdn_norm[li],
                             na_rpb[li], w_out[li], need_ctx)
        x = x + gt1 * y
        h2 = modulate(rms_norm(x, norm_ffn[li]), sh2, sc2)
        x = x + gt2 * expert_choice_ffn(h2, w_router[li], w_gate[li], w_up[li], w_down[li])
        if need_ctx:
            ctx = ctx + gt1c * y_c
            hc2 = modulate(rms_norm(ctx, norm_ffn[li]), sh2c, sc2c)
            ctx = ctx + gt2c * expert_choice_ffn(hc2, w_router[li], w_gate[li], w_up[li], w_down[li])
    return rms_norm(x, final_norm)


DEPTH_2 = 2

N_META = 16
D_MIX = D_MODEL
D_POOL = D_MIX // 4
D_CONV = D_MIX // 4
D_RET = D_MIX - D_POOL - D_CONV
POOL_WINDOWS = (2, 4, 8, 16)
N_POOL_GROUPS = len(POOL_WINDOWS)
POOL_GROUP = D_POOL // N_POOL_GROUPS
CONV_WIDTH = 31
RET_HEADS = 4
RET_HEAD_DIM = D_RET // RET_HEADS
D_FF = ((8 * D_MODEL // 3 + 63) // 64) * 64
D_IN = D_POOL + 2 * D_CONV + 4 * D_RET
DEEPNORM_ALPHA = (2.0 * DEPTH_2) ** 0.25
DEEPNORM_BETA = (8.0 * DEPTH_2) ** -0.25
LN_EPS = 1e-5


def layer_norm(x, g, b):
    xf = x.astype(jnp.float32)
    mu = jnp.mean(xf, axis=-1, keepdims=True)
    var = jnp.mean(jnp.square(xf - mu), axis=-1, keepdims=True)
    return ((xf - mu) * lax.rsqrt(var + LN_EPS) * g + b).astype(x.dtype)

def swiglu_ffn(x, w13, w2):
    a, u = jnp.split(x @ w13, 2, axis=-1)
    return (jax.nn.silu(a) * u) @ w2

def pool_mixer(xp, w_pool, scale):
    B, L, _ = xp.shape
    xf = xp.astype(jnp.float32)
    cs = jnp.concatenate([jnp.zeros((B, 1, D_POOL), jnp.float32), jnp.cumsum(xf, axis=1)], axis=1)
    t = jnp.arange(L)
    outs = []
    for gi, w in enumerate(POOL_WINDOWS):
        lo, hi = gi * POOL_GROUP, (gi + 1) * POOL_GROUP
        csg = cs[..., lo:hi]
        start = jnp.maximum(t + 1 - w, 0)
        win_sum = csg[:, 1:] - csg[:, start]
        count = (t + 1 - start).astype(jnp.float32)
        outs.append(win_sum / count[None, :, None] - xf[..., lo:hi])
    y = jnp.stack(outs, axis=2)
    y = jnp.einsum('blgc,gcd->blgd', y, w_pool.astype(jnp.float32)).reshape(B, L, D_POOL)
    return (y * scale).astype(xp.dtype)

def conv_module(a, gate, w_dw, b_dw, ln_g, ln_b, w_pw):
    u = a * jax.nn.sigmoid(gate)
    y = lax.conv_general_dilated(u, w_dw[:, None, :], window_strides=(1,),
                                 padding=[(CONV_WIDTH - 1, 0)],
                                 dimension_numbers=('NWC', 'WIO', 'NWC'),
                                 feature_group_count=D_CONV) + b_dw
    y = jax.nn.silu(layer_norm(y, ln_g, ln_b))
    return y @ w_pw

def rope(x, cos, sin):
    x1, x2 = jnp.split(x, 2, axis=-1)
    return jnp.concatenate([x1 * cos - x2 * sin, x2 * cos + x1 * sin], axis=-1)

def retention(q, k, v, g, gn_g):
    B, L, _ = q.shape
    f32 = jnp.float32
    pos = jnp.arange(L, dtype=f32)
    inv_freq = ROPE_BASE ** (-jnp.arange(0, RET_HEAD_DIM, 2, dtype=f32) / RET_HEAD_DIM)
    ang = pos[:, None] * inv_freq[None, :]
    cos, sin = jnp.cos(ang), jnp.sin(ang)
    heads = lambda t: t.astype(f32).reshape(B, L, RET_HEADS, RET_HEAD_DIM).transpose(0, 2, 1, 3)
    qh = rope(heads(q), cos, sin)
    kh = rope(heads(k), cos, sin) * (RET_HEAD_DIM ** -0.5)
    vh = heads(v)
    P = (-N_META) % CHUNK
    NC = (L + P) // CHUNK
    chunk = lambda t: jnp.pad(t, ((0, 0), (0, 0), (P, 0), (0, 0))).reshape(B, RET_HEADS, NC, CHUNK, RET_HEAD_DIM)
    qc, kc, vc = chunk(qh), chunk(kh), chunk(vh)
    log_gamma = jnp.log(1.0 - 2.0 ** (-5.0 - jnp.arange(RET_HEADS, dtype=f32)))
    i = jnp.arange(CHUNK, dtype=f32)
    intra_decay = jnp.exp(log_gamma[:, None, None] * jnp.abs(i[:, None] - i[None, :]))
    s = jnp.einsum('bhnid,bhnjd->bhnij', qc, kc) * intra_decay[None, :, None]
    o_intra = jnp.einsum('bhnij,bhnjd->bhnid', s, vc)
    q_decay = jnp.exp(log_gamma[:, None] * (i + 1.0))[None, :, :, None]
    k_decay = jnp.exp(log_gamma[:, None] * (CHUNK - 1.0 - i))[None, :, :, None]
    chunk_decay = jnp.exp(log_gamma * CHUNK)[None, :, None, None]

    def step(state, inp):
        q_n, k_n, v_n = inp
        o = jnp.einsum('bhid,bhde->bhie', q_n * q_decay, state)
        state = state * chunk_decay + jnp.einsum('bhjd,bhje->bhde', k_n * k_decay, v_n)
        return state, o

    to_scan = lambda t: t.transpose(2, 0, 1, 3, 4)
    state0 = jnp.zeros((B, RET_HEADS, RET_HEAD_DIM, RET_HEAD_DIM), f32)
    _, o_cross = lax.scan(step, state0, (to_scan(qc), to_scan(kc), to_scan(vc)))
    o = o_intra + o_cross.transpose(1, 2, 0, 3, 4)
    o = o.reshape(B, RET_HEADS, NC * CHUNK, RET_HEAD_DIM)[:, :, P:]
    mu = jnp.mean(o, axis=-1, keepdims=True)
    var = jnp.mean(jnp.square(o - mu), axis=-1, keepdims=True)
    o = ((o - mu) * lax.rsqrt(var + LN_EPS)).transpose(0, 2, 1, 3).reshape(B, L, D_RET) * gn_g
    return (jax.nn.silu(g.astype(f32)) * o).astype(g.dtype)

def token_mix(h, w_in, pool_w, pool_scale, conv_dw, conv_db, conv_ln_g, conv_ln_b, conv_pw, ret_gn_g, w_out):
    z = h @ w_in
    splits = [D_POOL, D_POOL + D_CONV, D_POOL + 2 * D_CONV,
              D_POOL + 2 * D_CONV + D_RET, D_POOL + 2 * D_CONV + 2 * D_RET,
              D_POOL + 2 * D_CONV + 3 * D_RET]
    xp, ca, cg, q, k, v, g = jnp.split(z, splits, axis=-1)
    y_pool = pool_mixer(xp, pool_w, pool_scale)
    y_conv = conv_module(ca, cg, conv_dw, conv_db, conv_ln_g, conv_ln_b, conv_pw)
    y_ret = retention(q, k, v, g, ret_gn_g)
    return jnp.concatenate([y_pool, y_conv, y_ret], axis=-1) @ w_out

def second_inputs(seed: int = 0) -> dict:
    key = jax.random.key(seed)
    ks = jax.random.split(key, 24)
    nrm = lambda k, shape, s: jax.random.normal(k, shape, jnp.float32) * s
    ones_n = lambda k, shape: 1.0 + 0.05 * jax.random.normal(k, shape, jnp.float32)
    return {
        "x": nrm(ks[0], (BATCH, SEQ, D_MODEL), 1.0),
        "meta": nrm(ks[1], (N_META, D_MODEL), 1.0),
        "ln_in_g": ones_n(ks[2], (D_MODEL,)),
        "ln_in_b": nrm(ks[3], (D_MODEL,), 0.02),
        "ffn1_w13": nrm(ks[4], (DEPTH_2, D_MODEL, 2 * D_FF), D_MODEL ** -0.5),
        "ffn1_w2": nrm(ks[5], (DEPTH_2, D_FF, D_MODEL), DEEPNORM_BETA * D_FF ** -0.5),
        "w_in": nrm(ks[6], (DEPTH_2, D_MODEL, D_IN), D_MODEL ** -0.5),
        "pool_w": nrm(ks[7], (DEPTH_2, N_POOL_GROUPS, POOL_GROUP, POOL_GROUP), POOL_GROUP ** -0.5),
        "pool_scale": ones_n(ks[8], (DEPTH_2, D_POOL)),
        "conv_dw": nrm(ks[9], (DEPTH_2, CONV_WIDTH, D_CONV), CONV_WIDTH ** -0.5),
        "conv_db": nrm(ks[10], (DEPTH_2, D_CONV), 0.02),
        "conv_ln_g": ones_n(ks[11], (DEPTH_2, D_CONV)),
        "conv_ln_b": nrm(ks[12], (DEPTH_2, D_CONV), 0.02),
        "conv_pw": nrm(ks[13], (DEPTH_2, D_CONV, D_CONV), D_CONV ** -0.5),
        "ret_gn_g": ones_n(ks[14], (DEPTH_2, D_RET)),
        "w_out": nrm(ks[15], (DEPTH_2, D_MIX, D_MODEL), DEEPNORM_BETA * D_MIX ** -0.5),
        "ffn2_w13": nrm(ks[16], (DEPTH_2, D_MODEL, 2 * D_FF), D_MODEL ** -0.5),
        "ffn2_w2": nrm(ks[17], (DEPTH_2, D_FF, D_MODEL), DEEPNORM_BETA * D_FF ** -0.5),
        "ln_g": ones_n(ks[18], (DEPTH_2, 3, D_MODEL)),
        "ln_b": nrm(ks[19], (DEPTH_2, 3, D_MODEL), 0.02),
    }

def second_block(x, meta, ln_in_g, ln_in_b, ffn1_w13, ffn1_w2, w_in, pool_w, pool_scale,
              conv_dw, conv_db, conv_ln_g, conv_ln_b, conv_pw, ret_gn_g, w_out,
              ffn2_w13, ffn2_w2, ln_g, ln_b):
    B = x.shape[0]
    h = jnp.concatenate([jnp.broadcast_to(meta[None].astype(x.dtype), (B, N_META, D_MODEL)), x], axis=1)
    h = layer_norm(h, ln_in_g, ln_in_b)
    for l in range(DEPTH_2):
        h = layer_norm(DEEPNORM_ALPHA * h + 0.5 * swiglu_ffn(h, ffn1_w13[l], ffn1_w2[l]), ln_g[l, 0], ln_b[l, 0])
        mix = token_mix(h, w_in[l], pool_w[l], pool_scale[l], conv_dw[l], conv_db[l],
                        conv_ln_g[l], conv_ln_b[l], conv_pw[l], ret_gn_g[l], w_out[l])
        h = layer_norm(DEEPNORM_ALPHA * h + mix, ln_g[l, 1], ln_b[l, 1])
        h = layer_norm(DEEPNORM_ALPHA * h + 0.5 * swiglu_ffn(h, ffn2_w13[l], ffn2_w2[l]), ln_g[l, 2], ln_b[l, 2])
    return h[:, N_META:]


def setup_inputs(seed=0):
    out = dict(first_inputs(seed))
    for name, value in second_inputs(seed + 1).items():
        if name != "x":
            out[name + "_2"] = value
    return out


def reference(
    x, c, ctx, c_ctx, w_mod, b_mod, norm_mix, norm_ffn, w_in, conv_qkv, a_log, dt_bias,
    gdn_norm, na_rpb, w_out, w_router, w_gate, w_up, w_down, final_norm, meta_2, ln_in_g_2,
    ln_in_b_2, ffn1_w13_2, ffn1_w2_2, w_in_2, pool_w_2, pool_scale_2, conv_dw_2, conv_db_2,
    conv_ln_g_2, conv_ln_b_2, conv_pw_2, ret_gn_g_2, w_out_2, ffn2_w13_2, ffn2_w2_2, ln_g_2,
    ln_b_2,
):
    x = first_block(
        x, c, ctx, c_ctx, w_mod, b_mod, norm_mix, norm_ffn, w_in, conv_qkv, a_log, dt_bias,
        gdn_norm, na_rpb, w_out, w_router, w_gate, w_up, w_down, final_norm,
    )
    return second_block(
        x, meta_2, ln_in_g_2, ln_in_b_2, ffn1_w13_2, ffn1_w2_2, w_in_2, pool_w_2, pool_scale_2,
        conv_dw_2, conv_db_2, conv_ln_g_2, conv_ln_b_2, conv_pw_2, ret_gn_g_2, w_out_2,
        ffn2_w13_2, ffn2_w2_2, ln_g_2, ln_b_2,
    )


_drawn_inputs = setup_inputs


def setup_inputs(seed=0):
    import zlib

    import numpy as np

    out = dict(_drawn_inputs(seed))
    spreads = {}
    factors = {'b_mod': 3.33,
     'norm_ffn': 2.715,
     'a_log': 3.447,
     'gdn_norm': 3.768,
     'na_rpb': 8.0,
     'pool_scale_2': 5.206,
     'conv_db_2': 8.0,
     'conv_ln_g_2': 6.159,
     'conv_ln_b_2': 8.0,
     'ret_gn_g_2': 5.336}
    for name, (base, spread) in spreads.items():
        noise = np.random.default_rng([zlib.crc32(name.encode()), seed]).standard_normal(out[name].shape)
        drawn = base * np.exp(spread * noise) if base else spread * noise
        out[name] = __import__('jax').numpy.asarray(drawn.astype(out[name].dtype))
    for name, factor in factors.items():
        out[name] = (out[name] * factor).astype(out[name].dtype)
    return out
```

```python
import numpy as np
import concourse.bass as bass
from concourse import mybir
from contextlib import ExitStack

F32 = mybir.dt.float32
U32 = mybir.dt.uint32
ALU = mybir.AluOpType
ACT = mybir.ActivationFunctionType
AX = mybir.AxisListType

P = 128
D = 1024
DK = D // P
T, TC = 512, 256
TT, TCT, NT = T // P, TC // P, (T + TC) // P
HG, DH = 4, 128
HN, DN = 8, 64
GRID = 64
ROWS = T // GRID
NROW, NCOL = 8, 16
CONV = 5
CHT = 4
EPS = 1e-6
SLOT = 4096
RING = 6
RING1 = 3
NE, CAP = 16, 64

NL, NMETA = 2, 16
L = T + NMETA
LH = L // 2
DFF = 2752
FT = -(-DFF // P)
W13C = FT // 2
W2C = DK
CW = 31
RH, RD = 4, 128
LN_EPS = 1e-5
ALPHA = 4.0 ** 0.25
TILES = [(0, NMETA)] + [(NMETA + P * i, P) for i in range(TT)]

MODC = 12
INC = 7
OUTC = 2
W1N = MODC + INC + OUTC
WEN = RING * NE
LAYC = 48



def table1():
    p = np.arange(P)[:, None]
    f = np.arange(P)[None, :]
    t = {"ident": p == f, "ones": np.ones((P, P)), "le": p <= f, "ge": p >= f, "lt": p < f, "gt": p > f}
    for d in range(2):
        for lev in range(7):
            b = 1 << lev
            m = (p // (2 * b) == f // (2 * b)) & (p // b != f // b) & (p > f)
            t[f"lev{d}_{lev}"] = m if d == 0 else m.T
    t["lev0_0T"], t["lev1_0T"] = t["lev1_0"], t["lev0_0"]
    tok = (np.arange(TT)[None, :] * P + np.arange(P)[:, None]).astype(np.float32)
    inv = (np.float32(10000.0) ** (-np.arange(32, dtype=np.float32) / np.float32(32))).astype(np.float32)
    row = np.floor(tok / GRID)[:, :, None] * inv
    col = (tok % GRID)[:, :, None] * inv
    cos = np.concatenate([np.cos(row), np.cos(row), np.cos(col), np.cos(col)], -1)
    sin = np.concatenate([-np.sin(row), np.sin(row), -np.sin(col), np.sin(col)], -1)
    t["cos"], t["sin"] = cos.reshape(P, -1), sin.reshape(P, -1)
    t["iota"] = np.broadcast_to(np.arange(CAP), (P, CAP))
    return {k: np.asarray(v, np.float32) for k, v in t.items()}


def table2():
    t = {}
    t["ident"] = np.eye(P)
    t["mean_d"] = np.full((P, P), 1.0 / D)
    t["mean_c"] = np.full((P, P), 1.0 / 256)
    t["mean_h"] = np.full((P, P), 1.0 / RD)
    pos = np.arange(L, dtype=np.float32)
    inv = (np.float32(10000.0) ** (-np.arange(0, RD, 2, dtype=np.float32) / np.float32(RD))).astype(np.float32)
    ang = np.concatenate([inv, inv])[:, None] * pos[None, :]
    t["cos"] = np.cos(ang)
    t["sin"] = np.concatenate([np.sin(ang[:64]), -np.sin(ang[64:])])
    p = np.arange(P)[:, None]
    x = np.arange(L)[None, :]
    lg = np.log(1.0 - 2.0 ** (-5.0 - np.arange(RH)))
    scale = float(RD) ** -0.5
    t["decay"] = np.concatenate([np.exp(g * np.abs(x - p)) * (x // 64 >= p // 64) * scale for g in lg], 1)
    cnt = np.zeros((P, 2, 16))
    for tile in range(2):
        for half in range(2):
            w = (2, 4, 8, 16)[tile * 2 + half]
            cnt[half * 64:half * 64 + 64, tile] = 1.0 / np.minimum(np.arange(16) + 1, w)
    t["cnt"] = cnt.reshape(P, 32)
    win = np.zeros((P, 2))
    for tile in range(2):
        for half in range(2):
            win[half * 64:half * 64 + 64, tile] = 1.0 / (2, 4, 8, 16)[tile * 2 + half]
    t["win"] = win
    return {k: np.asarray(v, np.float32) for k, v in t.items()}


def offsets(table):
    out, at = {}, 0
    for k, v in table.items():
        out[k] = (at, v.shape[1])
        at += v.shape[1]
    return out, at


class Map:

    def __init__(self, arena, start, end):
        self.arena, self.at, self.end = arena, start, end

    def take(self, *shape):
        n = int(np.prod(shape))
        assert self.at + n <= self.end, (self.at, n, self.end)
        v = self.arena[:, self.at:self.at + n]
        self.at += n
        if len(shape) == 2:
            v = v.rearrange("p (a b) -> p a b", a=shape[0])
        elif len(shape) == 3:
            v = v.rearrange("p (a b c) -> p a b c", a=shape[0], b=shape[1])
        return v


class PhaseSems:

    def __init__(self, nc):
        self.nc, self.stack, self.held = nc, ExitStack(), []

    def __call__(self, name):
        s = self.stack.enter_context(self.nc.semaphore(name))
        self.held.append(s)
        return s

    def close(self):
        with self.nc.Block() as block:
            @block.sync
            def _(sp):
                for s in self.held:
                    sp.sem_clear(s)
        self.stack.close()


def build(nc, A, out):
    with ExitStack() as ctx:
        def sem(name):
            return ctx.enter_context(nc.semaphore(name))

        TOTAL = 53100
        arena = ctx.enter_context(nc.sbuf_tensor("arena", [P, TOTAL], F32))
        PS = ctx.enter_context(nc.psum_tensor("PS", [P, 8, 512], F32))
        slots = [arena[:, s * SLOT:(s + 1) * SLOT] for s in range(RING)]
        arrived = [sem(f"arrived{s}") for s in range(RING)]
        used = sem("used")
        E = dict(nc=nc, A=A, out=out, sem=sem, arena=arena, PS=PS, slots=slots, arrived=arrived,
                 used=used, TOTAL=TOTAL)
        first_block(E)
        if PHASES > 5:
            second_block(E)


PHASES = 99


def first_block(E):
    nc, A, sem, arena, PS, slots = (E[k] for k in ("nc", "A", "sem", "arena", "PS", "slots"))
    arrived, used = E["arrived"], E["used"]
    o1, n1 = offsets(table1())
    B = Map(arena, RING * SLOT, E["TOTAL"])
    tab = B.take(n1)
    C = {k: tab[:, a:a + n] for k, (a, n) in o1.items()}
    ht_at = B.at
    hT = B.take(DK, NT * P)
    GT1, A2, SH2, GT2 = (B.take(D) for _ in range(4))
    sm = B.take(1000)
    yT = B.take(DK, T)
    rest_at = B.at

    def chunk_wait(eng, n):
        eng.wait_ge(arrived[n % RING1], 16 * (n // RING1 + 1))

    def load_chunk(sp, n):
        if n >= RING1:
            sp.wait_ge(used, n - RING1 + 1)
        sp.dma_start(slots[n % RING1], A["wts"][n, :, :]).then_inc(arrived[n % RING1], 16)

    S = Map(arena, RING1 * SLOT, RING * SLOT)
    bmod = S.take(MODC, 512)
    SH1, A1, SH1C, A1C = (S.take(D) for _ in range(4))
    nmix, nffn = S.take(D), S.take(D)
    R = Map(arena, rest_at, E["TOTAL"])
    xin = R.take(NT, D)
    crep = R.take(2 * DK, P)
    xsq = R.take(D)
    cv = sm[:, 0:16]
    cs = sm[:, 16:32]
    ss, rstd = sm[:, 32:38], sm[:, 40:46]
    tab_in, c_in, rows_in, x_in = sem("tab_in"), sem("c_in"), sem("rows_in"), sem("x_in")
    c_silu, c_rep, mod_ps, mod_sb = sem("c_silu"), sem("c_rep"), sem("mod_ps"), sem("mod_sb")
    sq_done, sq_sum, rms_sqrt, h_tok = sem("sq_done"), sem("sq_sum"), sem("rms_sqrt"), sem("h_tok")
    tr_ps, tr_free, tr_freev = sem("tr_ps"), sem("tr_free"), sem("tr_freev")
    OUTROW = [SH1, A1, GT1, SH2, A2, GT2]

    with nc.Block("modulate") as block:
        @block.sync
        def _(sp):
            for n in range(MODC + 3):
                load_chunk(sp, n)

        @block.scalar
        def _(act):
            act.dma_start(cv, A["cvec"]).then_inc(c_in, 16)
            act.dma_start(tab, A["tab1"]).then_inc(tab_in, 16)
            act.dma_start(bmod.rearrange("p a b -> p (a b)"), A["b_mod"].partition_broadcast(P)).then_inc(rows_in, 16)
            act.dma_start(nmix, A["norm_mix"].partition_broadcast(P)).then_inc(rows_in, 16)
            act.dma_start(nffn, A["norm_ffn"].partition_broadcast(P)).then_inc(rows_in, 16)
            act.dma_start(xin[:, 0:TCT, :], A["ctx"].rearrange("(t p) d -> p t d", p=P)).then_inc(x_in, 16)
            act.dma_start(xin[:, TCT:NT, :], A["x"].rearrange("(t p) d -> p t d", p=P)).then_inc(x_in, 16)
            act.wait_ge(c_in, 16)
            nc.scalar.activation(cs, cv, ACT.Silu).then_inc(c_silu, 1)
            act.wait_ge(x_in, 32)
            for t in range(NT):
                if t:
                    nc.scalar.drain()
                ins = nc.scalar.activation(xsq, xin[:, t, :], ACT.Square, accum_out=ss[:, t:t + 1])
            nc.scalar.drain().then_inc(sq_done, 1)
            act.wait_ge(sq_sum, 1)
            nc.scalar.activation(rstd, rstd, ACT.Sqrt).then_inc(rms_sqrt, 1)
            for g in range(NT * 2):
                if g % 2:
                    act.wait_ge(tr_ps, g + 1)
                    t, half = g // 2, g % 2
                    nc.scalar.activation(hT[:, half * 4:half * 4 + 4, t * P:(t + 1) * P],
                                         PS[:, g % 4, :].rearrange("p (a b) -> p a b", a=4), ACT.Copy).then_inc(tr_free, 1)

        @block.tensor
        def _(pe):
            pe.wait_ge(c_rep, 1)
            for j in range(MODC):
                chunk_wait(pe, j)
                if j >= 4:
                    pe.wait_ge(mod_sb, j - 3)
                w = slots[j % RING1].rearrange("p (k n) -> p k n", k=DK)
                for s in range(2 if j < 4 else 1):
                    for k in range(DK):
                        last = nc.tensor.matmul(PS[:, 2 * (j % 4) + s, :], crep[:, s * DK + k, :], w[:, k, :],
                                                start=(k == 0), stop=(k == DK - 1))
                last.then_inc(mod_ps, 1)
                nc.tensor.drain().then_inc(used, 1)
            pe.wait_ge(mod_sb, MODC)
            pe.wait_ge(tab_in, 16)
            for g in range(NT * 2):
                t, half = g // 2, g % 2
                if half == 0:
                    pe.wait_ge(h_tok, t + 1)
                if g >= 4:
                    pe.wait_ge(tr_free if g % 2 else tr_freev, (g - 4) // 2 + 1)
                for i in range(4):
                    k = half * 4 + i
                    last = nc.tensor.transpose(PS[:, g % 4, i * P:(i + 1) * P], xin[:, t, k * P:(k + 1) * P], C["ident"])
                last.then_inc(tr_ps, 1)

        @block.vector
        def _(dve):
            dve.wait_ge(c_silu, 1)
            nc.vector.tensor_copy(crep, cs.rearrange("p (a b) -> p a b", b=1).to_broadcast([P, 2 * DK, P])).then_inc(c_rep, 1)
            dve.wait_ge(sq_done, 1)
            nc.vector.tensor_scalar(rstd, ss, 1.0 / D, EPS, ALU.mult, ALU.add).then_inc(sq_sum, 1)
            dve.wait_ge(rms_sqrt, 1)
            nc.vector.reciprocal(rstd, rstd)
            dve.wait_ge(rows_in, 48)
            for j in range(MODC):
                dve.wait_ge(mod_ps, j + 1)
                row = OUTROW[j // 2][:, (j % 2) * 512:(j % 2 + 1) * 512]
                nc.vector.tensor_tensor(row, PS[:, 2 * (j % 4), :], bmod[:, j, :], ALU.add)
                if j < 4:
                    rowc = (SH1C, A1C)[j // 2][:, (j % 2) * 512:(j % 2 + 1) * 512]
                    nc.vector.tensor_tensor(rowc, PS[:, 2 * (j % 4) + 1, :], bmod[:, j, :], ALU.add)
                nc.vector.drain().then_inc(mod_sb, 1)
                if j // 2 in (1, 4):
                    nw = (nmix if j // 2 == 1 else nffn)[:, (j % 2) * 512:(j % 2 + 1) * 512]
                    nc.vector.scalar_tensor_tensor(row, row, 1.0, nw, ALU.add, ALU.mult)
                    if j // 2 == 1:
                        nc.vector.scalar_tensor_tensor(rowc, rowc, 1.0, nw, ALU.add, ALU.mult)
            nc.vector.drain()
            for t in range(NT):
                a, s = (A1C, SH1C) if t < TCT else (A1, SH1)
                nc.vector.scalar_tensor_tensor(xin[:, t, :], xin[:, t, :], rstd[:, t:t + 1], a, ALU.mult, ALU.mult)
                nc.vector.drain()
                nc.vector.tensor_tensor(xin[:, t, :], xin[:, t, :], s, ALU.add).then_inc(h_tok, 1)
            for g in range(0, NT * 2, 2):
                dve.wait_ge(tr_ps, g + 1)
                t = g // 2
                nc.vector.tensor_copy(hT[:, 0:4, t * P:(t + 1) * P],
                                      PS[:, g % 4, :].rearrange("p (a b) -> p a b", a=4)).then_inc(tr_freev, 1)

    if PHASES < 2:
        return
    attention(E, locals())
    if PHASES < 3:
        return
    delta_rule(E, locals())
    if PHASES < 4:
        return
    experts(E, locals())


def attention(E, V):
    nc, A, sem, arena, PS, slots = (E[k] for k in ("nc", "A", "sem", "arena", "PS", "slots"))
    used, C, hT, yT, sm = E["used"], V["C"], V["hT"], V["yT"], V["sm"]
    chunk_wait, load_chunk = V["chunk_wait"], V["load_chunk"]
    R = Map(arena, V["rest_at"], E["TOTAL"])
    nqT = R.take(CHT, T)
    nkT = R.take(CHT, NT * P)
    nv = R.take(NT, 512)
    S = Map(arena, RING1 * SLOT, RING * SLOT)
    bias = S.take(2, D)
    sc = S.take(2, T + TC)
    pT = S.take(2, NT * P)
    otok = S.take(TT, 512)
    mx, nm, rs, rr = sm[:, 0:4], sm[:, 4:6], sm[:, 8:12], sm[:, 12:16]
    pj_ps, pj_v, pj_a = sem("pj_ps"), sem("pj_v"), sem("pj_a")

    groups = [("q", m) for m in range(CHT)] + [("k", m) for m in range(CHT)] + [("v", t) for t in range(NT)]
    with nc.Block("na_project") as block:
        @block.sync
        def _(sp):
            for n in range(MODC + 3, MODC + 6):
                load_chunk(sp, n)

        @block.tensor
        def _(pe):
            for g, (kind, m) in enumerate(groups):
                ci = "qkv".index(kind)
                if m == 0:
                    chunk_wait(pe, MODC + ci)
                w = slots[(MODC + ci) % RING1].rearrange("p (k n) -> p k n", k=DK)
                if g >= 4:
                    pe.wait_ge(pj_a if g % 2 else pj_v, (g - 4) // 2 + 1)
                b = 2 * (g % 4)
                for k in range(DK):
                    st = dict(start=(k == 0), stop=(k == DK - 1))
                    if kind == "q":
                        last = nc.tensor.matmul(PS[:, b, :], w[:, k, m * P:(m + 1) * P], hT[:, k, TC:], **st)
                    elif kind == "k":
                        nc.tensor.matmul(PS[:, b, 0:384], w[:, k, m * P:(m + 1) * P], hT[:, k, 0:384], **st)
                        last = nc.tensor.matmul(PS[:, b + 1, 0:384], w[:, k, m * P:(m + 1) * P], hT[:, k, 384:], **st)
                    else:
                        last = nc.tensor.matmul(PS[:, b, :], hT[:, k, m * P:(m + 1) * P], w[:, k, :], **st)
                last.then_inc(pj_ps, 1)
                if m == (NT if kind == "v" else CHT) - 1:
                    nc.tensor.drain().then_inc(used, 1)

        def evacuate(eng, e, done, parity):
            for g, (kind, m) in enumerate(groups):
                if g % 2 != parity:
                    continue
                b = 2 * (g % 4)
                eng.wait_ge(pj_ps, g + 1)
                if kind == "q":
                    src, dst, f = PS[:, b, :], nqT[:, m, :], DN ** -0.5
                elif kind == "k":
                    src, dst, f = PS[:, b:b + 2, 0:384], nkT[:, m, :].rearrange("p (a b) -> p a b", a=2), 1.0
                else:
                    src, dst, f = PS[:, b, :], nv[:, m, :], 1.0
                e(dst, src, f).then_inc(done, 1)

        @block.vector
        def _(dve):
            evacuate(dve, lambda d, s, f: nc.vector.tensor_scalar(d, s, f, None, ALU.mult), pj_v, 0)

        @block.scalar
        def _(act):
            evacuate(act, lambda d, s, f: nc.scalar.activation(d, s, ACT.Copy, scale=f), pj_a, 1)

    bias_in = [sem("bias_in0"), sem("bias_in1")]
    bias_used, sc_ps, sc_bias, sc_exp = sem("bias_used"), sem("sc_ps"), sem("sc_bias"), sem("sc_exp")
    pt_ps, pt_v, pt_a, o_ps, o_sb = sem("pt_ps"), sem("pt_v"), sem("pt_a"), sem("o_ps"), sem("o_sb")
    yt_ps, yt_sb = sem("yt_ps"), sem("yt_sb")
    N = HN * TT
    with nc.Block("na_attend") as block:
        @block.sync
        def _(sp):
            for h in range(HN):
                if h >= 2:
                    sp.wait_ge(bias_used, TT * (h - 1))
                sp.dma_start(bias[:, h % 2, :], A["na_bias"][h, :, :]).then_inc(bias_in[h % 2], 16)

        @block.tensor
        def _(pe):
            for i in range(N + 2):
                if i < N:
                    h, a = divmod(i, TT)
                    if i >= 2:
                        pe.wait_ge(sc_exp, i - 1)
                    lo = (h % 2) * DN
                    q = nqT[lo:lo + DN, h // 2, a * P:(a + 1) * P]
                    b = 2 * (i % 2)
                    nc.tensor.matmul(PS[:, b, :], q, nkT[lo:lo + DN, h // 2, TC:], start=True, stop=True)
                    nc.tensor.matmul(PS[:, b + 1, 0:TC], q, nkT[lo:lo + DN, h // 2, 0:TC], start=True, stop=True).then_inc(sc_ps, 1)
                if 1 <= i <= N:
                    j = i - 1
                    pe.wait_ge(sc_exp, j + 1)
                    if j >= 1:
                        pe.wait_ge(pt_v, j)
                        pe.wait_ge(pt_a, j)
                    for t in range(NT):
                        last = nc.tensor.transpose(PS[:, 4 + t // 4, (t % 4) * P:(t % 4 + 1) * P],
                                                   sc[:, j % 2, t * P:(t + 1) * P], C["ident"])
                    last.then_inc(pt_ps, 1)
                if i >= 2:
                    j = i - 2
                    h = j // TT
                    pe.wait_ge(pt_v, j + 1)
                    pe.wait_ge(pt_a, j + 1)
                    if j >= 2:
                        pe.wait_ge(o_sb, j - 1)
                    for t in range(NT):
                        last = nc.tensor.matmul(PS[:, 6 + j % 2, 0:DN], pT[:, j % 2, t * P:(t + 1) * P],
                                                nv[:, t, h * DN:(h + 1) * DN], start=(t == 0), stop=(t == NT - 1))
                    last.then_inc(o_ps, 1)
            pe.wait_ge(o_sb, N)
            for a in range(TT):
                for k in range(4):
                    last = nc.tensor.transpose(PS[:, a, k * P:(k + 1) * P], otok[:, a, k * P:(k + 1) * P], C["ident"])
                last.then_inc(yt_ps, 1)

        @block.vector
        def _(dve):
            for i in range(N + 2):
                if i < N:
                    h, a = divmod(i, TT)
                    dve.wait_ge(sc_ps, i + 1)
                    if a == 0:
                        dve.wait_ge(bias_in[h % 2], 16 * (h // 2 + 1))
                    if i >= 2:
                        dve.wait_ge(pt_ps, i - 1)
                    b, m = 2 * (i % 2), 2 * (i % 2)
                    e0 = (7 - 2 * a) * GRID
                    nc.vector.tensor_tensor_reduce(out=sc[:, i % 2, TC:], in0=PS[:, b, :], in1=bias[:, h % 2, e0:e0 + T],
                                                   scale=1.0, scalar=-3e38, op0=ALU.add, op1=ALU.max,
                                                   accum_out=mx[:, m:m + 1]).then_inc(bias_used, 1)
                    nc.vector.reduce_max(mx[:, m + 1:m + 2], PS[:, b + 1, 0:TC], AX.X)
                    nc.vector.drain()
                    nc.vector.tensor_reduce(nm[:, i % 2:i % 2 + 1], mx[:, m:m + 2], AX.X, ALU.max, negate=True).then_inc(sc_bias, 1)
                if 1 <= i <= N:
                    j = i - 1
                    dve.wait_ge(pt_ps, j + 1)
                    if j >= 2:
                        dve.wait_ge(o_ps, j - 1)
                    nc.vector.tensor_copy(pT[:, j % 2, 0:512], PS[:, 4, :]).then_inc(pt_v, 1)
                if i >= 2:
                    j = i - 2
                    h, a = divmod(j, TT)
                    dve.wait_ge(o_ps, j + 1)
                    m = 2 * (j % 2)
                    nc.vector.tensor_tensor(rr[:, m:m + 1], rs[:, m:m + 1], rs[:, m + 1:m + 2], ALU.add)
                    nc.vector.drain()
                    nc.vector.reciprocal(rr[:, m + 1:m + 2], rr[:, m:m + 1])
                    nc.vector.drain()
                    nc.vector.tensor_scalar(otok[:, a, h * DN:(h + 1) * DN], PS[:, 6 + j % 2, 0:DN],
                                            rr[:, m + 1:m + 2], None, ALU.mult).then_inc(o_sb, 1)
            for a in range(TT):
                dve.wait_ge(yt_ps, a + 1)
                nc.vector.tensor_copy(yT[:, 4:8, a * P:(a + 1) * P],
                                      PS[:, a, :].rearrange("p (a b) -> p a b", a=4)).then_inc(yt_sb, 1)

        @block.scalar
        def _(act):
            for i in range(N + 1):
                if i < N:
                    act.wait_ge(sc_bias, i + 1)
                    if i >= 2:
                        act.wait_ge(o_sb, i - 1)
                    m = 2 * (i % 2)
                    nc.scalar.activation(sc[:, i % 2, 0:TC], PS[:, m + 1, 0:TC], ACT.Exp, bias=nm[:, i % 2:i % 2 + 1],
                                         accum_out=rs[:, m:m + 1])
                    nc.scalar.activation(sc[:, i % 2, TC:], sc[:, i % 2, TC:], ACT.Exp, bias=nm[:, i % 2:i % 2 + 1],
                                         accum_out=rs[:, m + 1:m + 2])
                    nc.scalar.drain().then_inc(sc_exp, 1)
                if i >= 1:
                    j = i - 1
                    act.wait_ge(pt_ps, j + 1)
                    if j >= 2:
                        act.wait_ge(o_ps, j - 1)
                    nc.scalar.activation(pT[:, j % 2, 512:768], PS[:, 5, 0:TC], ACT.Copy).then_inc(pt_a, 1)


def spread(ap, n):
    return ap.unsqueeze(2).to_broadcast([P, ap.shape[1], n])


def over(ap, h):
    return ap.unsqueeze(1).to_broadcast([P, h, ap.shape[1]])


def heads(ap, h=HG):
    return ap.rearrange("p (h d) -> p h d", h=h)


def delta_rule(E, V):
    nc, A, arena, PS, slots = (E[k] for k in ("nc", "A", "arena", "PS", "slots"))
    sem = PhaseSems(nc)
    used, C, hT, yT, sm = E["used"], V["C"], V["hT"], V["yT"], V["sm"]
    chunk_wait, load_chunk = V["chunk_wait"], V["load_chunk"]
    R = Map(arena, V["rest_at"], E["TOTAL"])
    ktok, qT, kT = R.take(NT, 512), R.take(HG, T), R.take(HG, NT * P)
    sq = R.take(2, 512)
    S = Map(arena, RING1 * SLOT, RING * SLOT)
    vtok, gate = S.take(NT, 512), S.take(TT, 512)
    s_at = S.at
    RAW = 2 + TC + 2 + T + 2
    OUTW = TC + 2 + T
    raw, acc, swapped = S.take(CHT, RAW), S.take(CHT, OUTW), S.take(512)
    qtok = yT[:, 0:4, :]
    wab = sm[:, 64:192].rearrange("p (k n) -> p k n", k=DK)
    convw = sm[:, 192:252].rearrange("p (c w) -> p c w", c=12)
    alog, dtb = sm[:, 256:264], sm[:, 264:272]
    ssn = sm[:, 272:296]
    g = sm[:, 300:348].rearrange("p (t n) -> p t n", t=NT)
    nb = sm[:, 348:396].rearrange("p (t n) -> p t n", t=NT)
    beta = sm[:, 396:444].rearrange("p (t n) -> p t n", t=NT)
    t0 = sm[:, 444:492].rearrange("p (t n) -> p t n", t=NT)
    gnw = sm[:, 492:620]

    small_in, gp_ps, gp_sb, conv_done, silu_done = (sem(x) for x in ("small_in", "gp_ps", "gp_sb", "conv_done", "silu_done"))
    tk_ps, tk_sb, sq_sb, ss_sb, nrm_ready, nrm_sqrt, tok_ready, pad_zero = (
        sem(x) for x in ("tk_ps", "tk_sb", "sq_sb", "ss_sb", "nrm_ready", "nrm_sqrt", "tok_ready", "pad_zero"))
    ab_ps, ab_z, ab_e = (sem(x) for x in ("ab_ps", "ab_z", "ab_e"))
    tok_sb = sem("tok_sb")

    proj = [("gate", t) for t in range(TT)] + [(c, m) for c in "qkv" for m in range(CHT)]
    tiles = {"q": list(range(TCT, NT)), "k": list(range(NT)), "v": list(range(NT))}
    trs = ([("T", "q", t) for t in tiles["q"]] + [("T", "k", t) for t in tiles["k"]] +
           [("B", "q", t) for t in tiles["q"]] + [("T", "v", t) for t in tiles["v"]] +
           [("B", "k", t) for t in tiles["k"]])
    tri = {x: i for i, x in enumerate(trs)}
    nT = {"q": 4, "k": 10, "v": 20}
    nt0 = {"q": 0, "k": 4}
    cidx = {"q": 0, "k": 1, "v": 2}

    def acc_col(t):
        return t * P if t < TCT else 2 + t * P

    with nc.Block("gdn_project") as block:
        @block.sync
        def _(sp):
            for n in range(MODC + 6, W1N):
                load_chunk(sp, n)

        @block.gpsimd
        def _(pool):
            nc.gpsimd.memset(raw, 0.0).then_inc(pad_zero, 1)
            for c in "qk":
                for t in tiles[c]:
                    i = nt0[c] + tiles[c].index(t)
                    pool.wait_ge(tok_sb, i + 1)
                    if i >= 2:
                        pool.wait_ge(ss_sb, i - 1)
                    src = qtok[:, t - TCT, :] if c == "q" else ktok[:, t, :]
                    nc.gpsimd.tensor_tensor(sq[:, i % 2, :], src, src, ALU.mult).then_inc(sq_sb, 1)

        @block.tensor
        def _(pe):
            def project(lo, hi):
                for gi in range(lo, hi):
                    c, m = proj[gi]
                    if m == 0:
                        n = MODC + 3 + ("gate", "q", "k", "v").index(c)
                        chunk_wait(pe, n)
                    w = slots[n % RING1].rearrange("p (k n) -> p k n", k=DK)
                    if gi >= 2:
                        pe.wait_ge(gp_sb, gi - 1)
                    b = 2 * (gi % 2)
                    for k in range(DK):
                        st = dict(start=(k == 0), stop=(k == DK - 1))
                        if c == "gate":
                            last = nc.tensor.matmul(PS[:, b, :], hT[:, k, TC + m * P:TC + (m + 1) * P], w[:, k, :], **st)
                        else:
                            if c != "q":
                                nc.tensor.matmul(PS[:, b + 1, 0:TC], w[:, k, m * P:(m + 1) * P], hT[:, k, 0:TC], **st)
                            last = nc.tensor.matmul(PS[:, b, :], w[:, k, m * P:(m + 1) * P], hT[:, k, TC:], **st)
                    last.then_inc(gp_ps, 1)
                    if m == 3:
                        nc.tensor.drain().then_inc(used, 1)

            def transposes(kind, c):
                if kind == "T":
                    pe.wait_ge(silu_done, CHT * (cidx[c] + 1))
                for t in tiles[c]:
                    u = tri[kind, c, t]
                    if kind == "B":
                        pe.wait_ge(tok_ready, nt0[c] + tiles[c].index(t) + 1)
                    if u >= 4:
                        pe.wait_ge(tk_sb, u - 3)
                    for m in range(CHT):
                        if kind == "T":
                            src = acc[:, m, acc_col(t):acc_col(t) + P]
                        else:
                            src = (qtok[:, t - TCT, :] if c == "q" else ktok[:, t, :])[:, m * P:(m + 1) * P]
                        last = nc.tensor.transpose(PS[:, 4 + u % 4, m * P:(m + 1) * P], src, C["ident"])
                    last.then_inc(tk_ps, 1)

            project(0, 4)
            pe.wait_ge(small_in, 16 * 5)
            for t in range(NT):
                for k in range(DK):
                    last = nc.tensor.matmul(PS[:, 7, 16 * t:16 * t + 16], hT[:, k, t * P:(t + 1) * P], wab[:, k, :],
                                            start=(k == 0), stop=(k == DK - 1))
            last.then_inc(ab_ps, 1)
            project(4, 12)
            pe.wait_ge(ab_z, 1)
            transposes("T", "q")
            project(12, 16)
            transposes("T", "k")
            transposes("B", "q")
            transposes("T", "v")
            transposes("B", "k")

        @block.scalar
        def _(act):
            act.dma_start(wab.rearrange("p k n -> p (k n)"), A["w_ab"]).then_inc(small_in, 16)
            act.dma_start(convw.rearrange("p c w -> p (c w)"), A["conv"]).then_inc(small_in, 16)
            act.dma_start(alog, A["a_log"].partition_broadcast(P)).then_inc(small_in, 16)
            act.dma_start(dtb, A["dt_bias"].partition_broadcast(P)).then_inc(small_in, 16)
            act.dma_start(gnw, A["gdn_norm"].partition_broadcast(P)).then_inc(small_in, 16)
            act.wait_ge(pad_zero, 1)

            def evac_proj(lo, hi):
                for gi in range(lo, hi):
                    c, m = proj[gi]
                    b = 2 * (gi % 2)
                    act.wait_ge(gp_ps, gi + 1)
                    if c == "gate":
                        nc.scalar.activation(gate[:, m, :], PS[:, b, :], ACT.Silu).then_inc(gp_sb, 1)
                    else:
                        if c != "q":
                            act.wait_ge(conv_done, CHT * (cidx[c] - 1) + m + 1)
                            nc.scalar.activation(raw[:, m, 2:2 + TC], PS[:, b + 1, 0:TC], ACT.Copy)
                        nc.scalar.activation(raw[:, m, 4 + TC:4 + TC + T], PS[:, b, :], ACT.Copy)
                        nc.scalar.drain().then_inc(gp_sb, 1)

            def silu(c):
                for m in range(CHT):
                    act.wait_ge(conv_done, CHT * cidx[c] + m + 1)
                    lo = 2 + TC if c == "q" else 0
                    nc.scalar.activation(acc[:, m, lo:], acc[:, m, lo:], ACT.Silu).then_inc(silu_done, 1)

            def evac_tr(kind, c):
                for t in tiles[c]:
                    u = tri[kind, c, t]
                    act.wait_ge(tk_ps, u + 1)
                    src = PS[:, 4 + u % 4, :]
                    if kind == "B":
                        dst = qT[:, :, (t - TCT) * P:(t - TCT + 1) * P] if c == "q" else kT[:, :, t * P:(t + 1) * P]
                        nc.scalar.activation(dst, heads(src), ACT.Copy).then_inc(tk_sb, 1)
                    else:
                        dst = qtok[:, t - TCT, :] if c == "q" else (ktok if c == "k" else vtok)[:, t, :]
                        nc.scalar.activation(dst, src, ACT.Copy)
                        nc.scalar.drain().then_inc(tk_sb, 1)
                        if c != "v":
                            nc.scalar.drain().then_inc(tok_sb, 1)

            def root(c):
                n = cidx[c] + 1
                act.wait_ge(nrm_ready, n)
                a, b = (0, 16) if c == "q" else (0, 24)
                nc.scalar.activation(ssn[:, a:b], ssn[:, a:b], ACT.Sqrt).then_inc(nrm_sqrt, 1)

            evac_proj(0, 4)
            evac_proj(4, 8)
            act.wait_ge(ab_z, 1)
            nc.scalar.activation(t0, g, ACT.Abs)
            nc.scalar.activation(beta, beta, ACT.Sigmoid)
            nc.scalar.activation(alog, alog, ACT.Exp)
            nc.scalar.drain()
            nc.scalar.activation(t0, t0, ACT.Exp, scale=-1.0)
            nc.scalar.drain()
            nc.scalar.activation(t0, t0, ACT.Ln, bias=1.0)
            nc.scalar.drain().then_inc(ab_e, 1)
            evac_proj(8, 12)
            silu("q")
            evac_tr("T", "q")
            evac_proj(12, 16)
            silu("k")
            evac_tr("T", "k")
            root("q")
            evac_tr("B", "q")
            silu("v")
            evac_tr("T", "v")
            root("k")
            evac_tr("B", "k")

        @block.vector
        def _(dve):
            dve.wait_ge(small_in, 16 * 5)
            dve.wait_ge(ab_ps, 1)
            ab = PS[:, 7, 0:16 * NT].rearrange("p (t n) -> p t n", t=NT)
            nc.vector.tensor_tensor(g, ab[:, :, 0:8], dtb.unsqueeze(1).to_broadcast([P, NT, 8]), ALU.add)
            nc.vector.tensor_copy(beta, ab[:, :, 8:16])
            nc.vector.drain().then_inc(ab_z, 1)

            def conv(c):
                ci = cidx[c]
                lo = 2 + TC if c == "q" else 0
                for m in range(CHT):
                    dve.wait_ge(gp_sb, 4 + CHT * ci + m + 1)
                    if ci and m == 0:
                        dve.wait_ge(tk_ps, {"k": 4, "v": 10}[c])
                    for w in range(CONV):
                        if w:
                            nc.vector.drain()
                        src, dst, k = raw[:, m, lo + w:OUTW + w], acc[:, m, lo:], convw[:, CHT * ci + m, w:w + 1]
                        if w == 0:
                            last = nc.vector.tensor_scalar(dst, src, k, None, ALU.mult)
                        else:
                            last = nc.vector.scalar_tensor_tensor(dst, src, k, dst, ALU.mult, ALU.add)
                    last.then_inc(conv_done, 1)

            def norm(c):
                n = len(tiles[c])
                for t in range(n):
                    i = nt0[c] + t
                    dve.wait_ge(sq_sb, i + 1)
                    nc.vector.reduce_sum(ssn[:, 4 * t:4 * t + 4], heads(sq[:, i % 2, :]), AX.X).then_inc(ss_sb, 1)
                nc.vector.drain()
                nc.vector.tensor_scalar(ssn[:, 0:4 * n], ssn[:, 0:4 * n], EPS, None, ALU.add).then_inc(nrm_ready, 1)
                dve.wait_ge(nrm_sqrt, cidx[c] + 1)
                nc.vector.reciprocal(ssn[:, 0:4 * n], ssn[:, 0:4 * n])
                nc.vector.drain()
                if c == "q":
                    nc.vector.tensor_scalar(ssn[:, 0:4 * n], ssn[:, 0:4 * n], DH ** -0.5, None, ALU.mult)
                    nc.vector.drain()
                for t in range(n):
                    x = qtok[:, t, :] if c == "q" else ktok[:, t, :]
                    nc.vector.tensor_tensor(heads(x), heads(x), spread(ssn[:, 4 * t:4 * t + 4], P), ALU.mult)
                    lt = tiles[c][t] - TCT
                    if lt >= 0:
                        nc.vector.drain()
                        cos, sin = (heads(C[k], TT)[:, lt, :] for k in ("cos", "sin"))
                        sv, xv = (v.rearrange("p (h f j i) -> p h f j i", h=HG, f=2, j=2) for v in (swapped, x))
                        sn = sin.rearrange("p (f j i) -> p f j i", f=2, j=2)
                        for j in range(2):
                            for f in range(2):
                                nc.vector.tensor_tensor(sv[:, :, f, j, :], xv[:, :, f, 1 - j, :],
                                                        sn[:, f, j, :].unsqueeze(1).to_broadcast([P, HG, 32]), ALU.mult)
                        nc.vector.drain()
                        nc.vector.tensor_tensor(heads(x), heads(x), over(cos, HG), ALU.mult)
                        nc.vector.drain()
                        nc.vector.tensor_tensor(x, x, swapped, ALU.add)
                    nc.vector.drain().then_inc(tok_ready, 1)

            conv("q")
            dve.wait_ge(ab_e, 1)
            nc.vector.scalar_tensor_tensor(g.rearrange("p t n -> p (t n)"), g.rearrange("p t n -> p (t n)"), 0.0,
                                           t0.rearrange("p t n -> p (t n)"), ALU.max, ALU.add)
            nc.vector.tensor_scalar(nb.rearrange("p t n -> p (t n)"), beta.rearrange("p t n -> p (t n)"), -1.0, None, ALU.mult)
            nc.vector.tensor_scalar(alog, alog, -1.0, None, ALU.mult)
            nc.vector.drain()
            nc.vector.tensor_tensor(g, g, alog.unsqueeze(1).to_broadcast([P, NT, 8]), ALU.mult)
            conv("k")
            norm("q")
            conv("v")
            norm("k")

    W = [Map(arena, s_at, RING * SLOT), Map(arena, V["ht_at"], V["ht_at"] + DK * NT * P)]
    names = ("GA", "DX", "AT", "LW", "LT", "XT", "vb", "kbe", "kd", "qv", "qdT", "St")
    B = [{k: heads(W[d].take(512)) for k in names} for d in range(2)]
    otok = W[0].take(2 * 512)
    ot2 = sq.rearrange("p a b -> p (a b)")
    o_at = [otok[:, 0:512], otok[:, 512:1024], ot2[:, 0:512], ot2[:, 512:1024]]
    ORDER = [list(range(NT)), [1, 0, 5, 4, 3, 2]]
    INC, STRICT_G, STRICT_L, BACK = ["le", "ge"], ["gt", "lt"], ["gt", "lt"], ["gt", "lt"]
    nq = 24
    eg, ed, gl, nbe = (sm[:, 620 + 48 * i:668 + 48 * i] for i in range(4))
    NS = 6

    def col(x, d, t):
        return x[:, d * nq + t * HG:d * nq + t * HG + HG]

    pre_ps, pre_sb = sem("pre_ps"), sem("pre_sb")
    pre_ready = sem("pre_ready")
    (g_sb, k_sb, dm_sb, x0_sb, d_sb, lt_sb, w_sb, vn_sb, o_cp, l_sb, xt0_sb, a_sb, x_sb, at_sb, s_sb, o_add, d_ps, kk_ps, lt_ps,
     a_ps, x_ps, w_ps, vn_ps, o_ps, ds_ps) = ([sem(f"{x}{d}") for d in range(2)] for x in (
         "g_sb", "k_sb", "dm_sb", "x0_sb", "d_sb", "lt_sb", "w_sb", "vn_sb", "o_cp", "l_sb", "xt0_sb", "a_sb", "x_sb",
         "at_sb", "s_sb", "o_add", "d_ps", "kk_ps", "lt_ps", "a_ps", "x_ps", "w_ps", "vn_ps", "o_psd", "ds_ps"))
    fin_sq, fin_ss, fin_rt, fin_o, fin_ps = (sem(x) for x in ("fin_sq", "fin_ss", "fin_rt", "fin_o", "fin_ps"))

    with nc.Block("delta") as block:
        @block.gpsimd
        def _(pool):
            pool.wait_ge(pre_ready, 1)
            for s in range(NT):
                for d in range(2):
                    if s:
                        pool.wait_ge(x_ps[d], NS * s)
                    t = ORDER[d][s]
                    nc.gpsimd.tensor_tensor(B[d]["GA"], spread(g[:, t, d * HG:d * HG + HG], P), over(C[STRICT_G[d]], HG),
                                            ALU.mult).then_inc(g_sb[d], 1)
                for d in range(2):
                    t, b = ORDER[d][s], B[d]
                    if s:
                        pool.wait_ge(ds_ps[d], s)
                    nc.gpsimd.tensor_tensor(b["vb"], heads(vtok[:, t, :]), spread(beta[:, t, d * HG:d * HG + HG], P), ALU.mult)
                    nc.gpsimd.tensor_tensor(b["kbe"], heads(ktok[:, t, :]), spread(col(nbe, d, t), P), ALU.mult)
                    last = nc.gpsimd.tensor_tensor(b["kd"], heads(ktok[:, t, :]), spread(col(ed, d, t), P), ALU.mult)
                    if t >= TCT:
                        nc.gpsimd.tensor_tensor(b["qv"], heads(qtok[:, t - TCT, :]), spread(col(eg, d, t), P), ALU.mult)
                    nc.gpsimd.drain().then_inc(k_sb[d], 1)
                for d in range(2):
                    t, b = ORDER[d][s], B[d]
                    pool.wait_ge(d_sb[d], s + 1)
                    nc.gpsimd.tensor_tensor(b["DX"], b["DX"], over(C[STRICT_L[d]], HG), ALU.mult)
                    if t >= TCT:
                        nc.gpsimd.tensor_tensor(b["AT"], b["AT"], over(C[INC[d]], HG), ALU.mult)
                    nc.gpsimd.drain()
                    nc.gpsimd.tensor_tensor(b["DX"], b["DX"], spread(nb[:, t, d * HG:d * HG + HG], P), ALU.mult)
                    nc.gpsimd.drain().then_inc(dm_sb[d], 1)
                for d in range(2):
                    b = B[d]
                    pool.wait_ge(l_sb[d], s + 1)
                    nc.gpsimd.tensor_tensor(b["DX"], b["LW"], over(C[f"lev{d}_0"], HG), ALU.mult)
                    nc.gpsimd.drain()
                    nc.gpsimd.tensor_tensor(b["DX"], b["DX"], over(C["ident"], HG), ALU.add).then_inc(x0_sb[d], 1)
            pool.wait_ge(o_add[0], 2)
            pool.wait_ge(o_add[1], 2)
            for t in range(TT):
                nc.gpsimd.tensor_tensor(B[0][("GA", "DX", "AT", "LW")[t]], heads(o_at[t]), heads(o_at[t]), ALU.mult)
            nc.gpsimd.drain().then_inc(fin_sq, 1)

        @block.tensor
        def _(pe):
            for d in range(2):
                gd = g[:, :, d * HG:d * HG + HG]
                for i, m in enumerate((INC[d], BACK[d], "ones")):
                    last = nc.tensor.matmul(PS[:, d, i * nq:(i + 1) * nq].rearrange("p (t h) -> p t h", t=NT), C[m], gd,
                                            start=True, stop=True)
            last.then_inc(pre_ps, 1)
            pe.wait_ge(pre_sb, 1)
            for s in range(NT):
                for d in range(2):
                    t, b, q = ORDER[d][s], B[d], 4 * d
                    pe.wait_ge(g_sb[d], s + 1)
                    if s:
                        pe.wait_ge(s_sb[d], s)
                    if s > 2:
                        pe.wait_ge((o_cp if s <= 4 else o_add)[d], s - 2 if s <= 4 else s - 4)
                    last = nc.tensor.matmul(PS[:, q, :], C[INC[d]], b["GA"].rearrange("p h d -> p (h d)"), start=True, stop=True)
                    if t >= TCT:
                        for h in range(HG):
                            last = nc.tensor.matmul(PS[:, q + 1, h * P:(h + 1) * P], b["GA"][:, h, :], C[INC[d]], start=True, stop=True)
                    last.then_inc(d_ps[d], 1)
                    for h in range(HG):
                        kh = kT[:, h, t * P:(t + 1) * P]
                        last = nc.tensor.matmul(PS[:, q + 2, h * P:(h + 1) * P], kh, kh, start=True, stop=True)
                    last.then_inc(kk_ps[d], 1)
                for d in range(2):
                    b, q = B[d], 4 * d
                    pe.wait_ge(l_sb[d], s + 1)
                    for h in range(HG):
                        last = nc.tensor.transpose(PS[:, q + 3, h * P:(h + 1) * P], b["LW"][:, h, :], C["ident"])
                    last.then_inc(lt_ps[d], 1)
                for lev in range(1, NS + 1):
                    for d in range(2):
                        b, q = B[d], 4 * d
                        if lev == 1:
                            pe.wait_ge(lt_sb[d], s + 1)
                            pe.wait_ge(x0_sb[d], s + 1)
                            pe.wait_ge(xt0_sb[d], s + 1)
                        else:
                            pe.wait_ge(x_sb[d], NS * s + lev - 1)
                        for h in range(HG):
                            last = nc.tensor.matmul(PS[:, q, h * P:(h + 1) * P], b["LT"][:, h, :], b["DX"][:, h, :], start=True, stop=True)
                        last.then_inc(a_ps[d], 1)
                    for d in range(2):
                        b, q = B[d], 4 * d
                        pe.wait_ge(a_sb[d], NS * s + lev)
                        for h in range(HG):
                            if lev < NS:
                                nc.tensor.matmul(PS[:, q + 1, h * P:(h + 1) * P], b["XT"][:, h, :], b["GA"][:, h, :], start=True, stop=True)
                            last = nc.tensor.matmul(PS[:, q + 2, h * P:(h + 1) * P], b["GA"][:, h, :], b["XT"][:, h, :], start=True, stop=True)
                        last.then_inc(x_ps[d], 1)
                for d in range(2):
                    t, b, q = ORDER[d][s], B[d], 4 * d
                    pe.wait_ge(x_sb[d], NS * s + NS)
                    pe.wait_ge(k_sb[d], s + 1)
                    for h in range(HG):
                        last = nc.tensor.matmul(PS[:, q, h * P:(h + 1) * P], b["kbe"][:, h, :], b["XT"][:, h, :], start=True, stop=True)
                    if t >= TCT:
                        for h in range(HG):
                            nc.tensor.matmul(PS[:, q + 1, h * P:(h + 1) * P], kT[:, h, t * P:(t + 1) * P],
                                             qT[:, h, (t - TCT) * P:(t - TCT + 1) * P], start=True, stop=True)
                            last = nc.tensor.transpose(PS[:, q + 2, h * P:(h + 1) * P], b["qv"][:, h, :], C["ident"])
                    last.then_inc(w_ps[d], 1)
                for d in range(2):
                    b, q = B[d], 4 * d
                    pe.wait_ge(w_sb[d], s + 1)
                    for h in range(HG):
                        dst = PS[:, q + 3, h * P:(h + 1) * P]
                        last = nc.tensor.matmul(dst, b["XT"][:, h, :], b["vb"][:, h, :], start=True, stop=(s == 0))
                        if s:
                            last = nc.tensor.matmul(dst, b["LW"][:, h, :], b["St"][:, h, :], start=False, stop=True)
                    last.then_inc(vn_ps[d], 1)
                for d in range(2):
                    t, b, q = ORDER[d][s], B[d], 4 * d
                    pe.wait_ge(vn_sb[d], s + 1)
                    if t >= TCT:
                        pe.wait_ge(at_sb[d], s - 1)
                        for h in range(HG):
                            dst = PS[:, q, h * P:(h + 1) * P]
                            nc.tensor.matmul(dst, b["qdT"][:, h, :], b["St"][:, h, :], start=True, stop=False)
                            last = nc.tensor.matmul(dst, b["AT"][:, h, :], b["qv"][:, h, :], start=False, stop=True)
                        last.then_inc(o_ps[d], 1)
                    for h in range(HG):
                        last = nc.tensor.matmul(PS[:, q + 1, h * P:(h + 1) * P], b["kd"][:, h, :], b["qv"][:, h, :], start=True, stop=True)
                    last.then_inc(ds_ps[d], 1)
            pe.wait_ge(fin_o, 1)
            for t in range(TT):
                for h in range(HG):
                    last = nc.tensor.transpose(PS[:, t, h * P:(h + 1) * P], o_at[t][:, h * P:(h + 1) * P], C["ident"])
                last.then_inc(fin_ps, 1)

        @block.scalar
        def _(act):
            act.wait_ge(pre_ps, 1)
            for d in range(2):
                for i, x in enumerate((eg, ed, gl)):
                    nc.scalar.activation(x[:, d * nq:(d + 1) * nq], PS[:, d, i * nq:(i + 1) * nq], ACT.Exp)
            nc.scalar.drain().then_inc(pre_sb, 1)
            for s in range(NT):
                for d in range(2):
                    t, b, q = ORDER[d][s], B[d], 4 * d
                    act.wait_ge(d_ps[d], s + 1)
                    nc.scalar.activation(b["DX"], heads(PS[:, q, :]), ACT.Exp)
                    if t >= TCT:
                        nc.scalar.activation(b["AT"], heads(PS[:, q + 1, :]), ACT.Exp)
                    nc.scalar.drain().then_inc(d_sb[d], 1)
                for d in range(2):
                    act.wait_ge(lt_ps[d], s + 1)
                    nc.scalar.activation(B[d]["LT"], heads(PS[:, 4 * d + 3, :]), ACT.Copy).then_inc(lt_sb[d], 1)
                for d in range(2):
                    t, b, q = ORDER[d][s], B[d], 4 * d
                    act.wait_ge(w_ps[d], s + 1)
                    nc.scalar.activation(b["LW"], heads(PS[:, q, :]), ACT.Copy)
                    if t >= TCT:
                        nc.scalar.activation(b["qdT"], heads(PS[:, q + 2, :]), ACT.Copy)
                    nc.scalar.drain().then_inc(w_sb[d], 1)
                for d in range(2):
                    act.wait_ge(vn_ps[d], s + 1)
                    nc.scalar.activation(B[d]["qv"], heads(PS[:, 4 * d + 3, :]), ACT.Copy).then_inc(vn_sb[d], 1)
                if 2 <= s <= 3:
                    for d in range(2):
                        act.wait_ge(o_ps[d], s - 1)
                        nc.scalar.activation(o_at[ORDER[d][s] - TCT], PS[:, 4 * d, :], ACT.Copy).then_inc(o_cp[d], 1)
            act.wait_ge(fin_ss, 1)
            nc.scalar.activation(ssn[:, 0:16], ssn[:, 0:16], ACT.Sqrt).then_inc(fin_rt, 1)

        @block.vector
        def _(dve):
            dve.wait_ge(pre_sb, 1)
            for d in range(2):
                nc.vector.tensor_tensor(nbe[:, d * nq:(d + 1) * nq].rearrange("p (t h) -> p t h", t=NT),
                                        eg[:, d * nq:(d + 1) * nq].rearrange("p (t h) -> p t h", t=NT),
                                        nb[:, :, d * HG:d * HG + HG], ALU.mult)
            nc.vector.drain().then_inc(pre_ready, 1)
            for s in range(NT):
                for d in range(2):
                    b, q = B[d], 4 * d
                    dve.wait_ge(kk_ps[d], s + 1)
                    dve.wait_ge(dm_sb[d], s + 1)
                    nc.vector.tensor_tensor(b["LW"], heads(PS[:, q + 2, :]), b["DX"], ALU.mult).then_inc(l_sb[d], 1)
                for d in range(2):
                    b, q = B[d], 4 * d
                    dve.wait_ge(lt_sb[d], s + 1)
                    nc.vector.tensor_tensor(b["XT"], b["LT"], over(C[f"lev{d}_0T"], HG), ALU.mult)
                    nc.vector.drain()
                    nc.vector.tensor_tensor(b["XT"], b["XT"], over(C["ident"], HG), ALU.add).then_inc(xt0_sb[d], 1)
                for lev in range(1, NS + 1):
                    for d in range(2):
                        b, q = B[d], 4 * d
                        dve.wait_ge(a_ps[d], NS * s + lev)
                        nc.vector.tensor_tensor(b["GA"], heads(PS[:, q, :]), over(C[f"lev{d}_{lev}"], HG), ALU.mult).then_inc(a_sb[d], 1)
                    for d in range(2):
                        b, q = B[d], 4 * d
                        dve.wait_ge(x_ps[d], NS * s + lev)
                        if lev < NS:
                            nc.vector.tensor_tensor(b["DX"], b["DX"], heads(PS[:, q + 1, :]), ALU.add)
                        nc.vector.tensor_tensor(b["XT"], b["XT"], heads(PS[:, q + 2, :]), ALU.add)
                        nc.vector.drain().then_inc(x_sb[d], 1)
                if s >= 2:
                    for d in range(2):
                        b, q = B[d], 4 * d
                        dve.wait_ge(w_ps[d], s + 1)
                        nc.vector.tensor_tensor(b["AT"], heads(PS[:, q + 1, :]), b["AT"], ALU.mult).then_inc(at_sb[d], 1)
                for d in range(2):
                    t, b, q = ORDER[d][s], B[d], 4 * d
                    if s >= 4:
                        dve.wait_ge(o_ps[d], s - 1)
                        dve.wait_ge(o_cp[1 - d], 2)
                        o = o_at[t - TCT]
                        nc.vector.tensor_tensor(o, o, PS[:, q, :], ALU.add).then_inc(o_add[d], 1)
                    dve.wait_ge(ds_ps[d], s + 1)
                    if s == 0:
                        nc.vector.tensor_copy(b["St"], heads(PS[:, q + 1, :])).then_inc(s_sb[d], 1)
                    else:
                        for h in range(HG):
                            i = d * nq + t * HG + h
                            nc.vector.scalar_tensor_tensor(b["St"][:, h, :], b["St"][:, h, :], gl[:, i:i + 1],
                                                           PS[:, q + 1, h * P:(h + 1) * P], ALU.mult, ALU.add)
                        nc.vector.drain().then_inc(s_sb[d], 1)
            dve.wait_ge(fin_sq, 1)
            for t in range(TT):
                nc.vector.reduce_sum(ssn[:, 4 * t:4 * t + 4], B[0][("GA", "DX", "AT", "LW")[t]], AX.X)
            nc.vector.drain()
            nc.vector.tensor_scalar(ssn[:, 0:16], ssn[:, 0:16], 1.0 / DH, EPS, ALU.mult, ALU.add).then_inc(fin_ss, 1)
            dve.wait_ge(fin_rt, 1)
            nc.vector.reciprocal(ssn[:, 0:16], ssn[:, 0:16])
            nc.vector.drain()
            for t in range(TT):
                o = heads(o_at[t])
                for f in (spread(ssn[:, 4 * t:4 * t + 4], P), over(gnw, HG), heads(gate[:, t, :])):
                    nc.vector.tensor_tensor(o, o, f, ALU.mult)
                    nc.vector.drain()
            nc.vector.drain().then_inc(fin_o, 1)
            for t in range(TT):
                dve.wait_ge(fin_ps, t + 1)
                nc.vector.tensor_copy(yT[:, 0:4, t * P:(t + 1) * P], heads(PS[:, t, :]))
    sem.close()


def experts(E, V):
    nc, A, arena, PS, slots = (E[k] for k in ("nc", "A", "arena", "PS", "slots"))
    sem = PhaseSems(nc)
    used, arrived, C, yT, sm = E["used"], E["arrived"], V["C"], V["yT"], V["sm"]
    GT1, A2, SH2, GT2 = V["GT1"], V["A2"], V["SH2"], V["GT2"]
    chunk_wait = V["chunk_wait"]
    R = Map(arena, V["rest_at"], E["TOTAL"])
    x1, h2 = R.take(TT, D), R.take(TT, D)
    H = Map(arena, V["ht_at"], V["ht_at"] + DK * NT * P)
    onehot = H.take(TT, NE * CAP)
    xe, hidT = H.take(DK, 2 * CAP), H.take(DK, 2 * CAP)
    wcur = R.take(512)
    h2T, WT = yT, yT
    WTp = yT
    ye, hs, hid = GT1, A2, SH2
    S = Map(arena, RING1 * SLOT, RING * SLOT)
    onew = S.take(TT, NE * CAP)
    affT, work, code = S.take(T), S.take(T), S.take(T)
    tmp = S.take(2, 512)
    sqs = S.take(D)
    wr = sm[:, 64:192].rearrange("p (k n) -> p k n", k=DK)
    ss, rstd = sm[:, 0:4], sm[:, 4:8]
    aff = sm[:, 192:256].rearrange("p (t e) -> p t e", t=TT)
    m4, codet = sm[:, 8:12], sm[:, 256:320].rearrange("p (t e) -> p t e", t=TT)
    top8 = sm[:, 320:328]

    x_in2, r_in, y_ps, y_sb, x1_done, ss_done, rt, h2_done = (sem(x) for x in (
        "x_in2", "r_in", "y_ps", "y_sb", "x1_done", "ss_done", "rt", "h2_done"))
    ht_ps, ht_sb, lg_ps, lg_ready, aff_e, aff_done, aft_ps, aft_sb, code_done, ct_ps, oh_sb, w_done, wt_ps, wt_sb, code_zero = (
        sem(x) for x in ("ht_ps", "ht_sb", "lg_ps", "lg_ready", "aff_e", "aff_done", "aft_ps", "aft_sb", "code_done",
                         "ct_ps", "oh_sb", "w_done", "wt_ps", "wt_sb", "code_zero"))

    def load_expert_chunk(sp, n, s):
        sp.dma_start(slots[s], A["wts"][bass.ds(W1N + RING * n + s, 1), :, :].rearrange("a p n -> (a p) n")).then_inc(arrived[s], 16)

    with nc.Block("route") as block:
        @block.sync
        def _(sp):
            sp.dma_start(x1, A["x"].rearrange("(t p) d -> p t d", p=P)).then_inc(x_in2, 16)
            sp.dma_start(wr.rearrange("p k n -> p (k n)"), A["w_router"]).then_inc(r_in, 16)
            for s in range(RING1):
                sp.wait_ge(used, W1N - RING1 + 1 + s)
                load_expert_chunk(sp, 0, s)

        @block.gpsimd
        def _(pool):
            nc.gpsimd.memset(code, 0.0).then_inc(code_zero, 1)
            for t in range(TT):
                pool.wait_ge(oh_sb, t + 1)
                last = nc.gpsimd.tensor_tensor(heads(onew[:, t, :], NE), heads(onehot[:, t, :], NE), spread(aff[:, t, :], CAP), ALU.mult)
                last.then_inc(w_done, 1)

        @block.tensor
        def _(pe):
            for hf in range(OUTC):
                n = MODC + INC + hf
                chunk_wait(pe, n)
                w = slots[n % RING1].rearrange("p (k n) -> p k n", k=DK)
                for t in range(TT):
                    for k in range(DK):
                        last = nc.tensor.matmul(PS[:, hf * 4 + t, :], yT[:, k, t * P:(t + 1) * P], w[:, k, :],
                                                start=(k == 0), stop=(k == DK - 1))
                    last.then_inc(y_ps, 1)
                nc.tensor.drain().then_inc(used, 1)
            for g in range(TT * 2):
                t, half = divmod(g, 2)
                if half == 0:
                    pe.wait_ge(h2_done, t + 1)
                if g >= 4:
                    pe.wait_ge(ht_sb, g - 3)
                for i in range(4):
                    k = half * 4 + i
                    last = nc.tensor.transpose(PS[:, g % 4, i * P:(i + 1) * P], h2[:, t, k * P:(k + 1) * P], C["ident"])
                last.then_inc(ht_ps, 1)
            pe.wait_ge(ht_sb, TT * 2)
            pe.wait_ge(r_in, 16)
            for t in range(TT):
                for k in range(DK):
                    last = nc.tensor.matmul(PS[:, 4, NE * t:NE * (t + 1)], h2T[:, k, t * P:(t + 1) * P], wr[:, k, :],
                                            start=(k == 0), stop=(k == DK - 1))
            last.then_inc(lg_ps, 1)
            pe.wait_ge(aff_done, 1)
            for t in range(TT):
                last = nc.tensor.transpose(PS[0:NE, 5, t * P:(t + 1) * P], aff[:, t, :], C["ident"])
            last.then_inc(aft_ps, 1)
            pe.wait_ge(code_done, 1)
            for t in range(TT):
                last = nc.tensor.transpose(PS[:, 6, t * P:(t + 1) * P], code[:, t * P:(t + 1) * P], C["ident"])
            last.then_inc(ct_ps, 1)
            pe.wait_ge(w_done, TT)
            for i in range(NE // 2):
                if i >= 4:
                    pe.wait_ge(wt_sb, i - 3)
                for t in range(TT):
                    last = nc.tensor.transpose(PS[:, i % 4, t * P:(t + 1) * P], onew[:, t, i * P:(i + 1) * P], C["ident"])
                last.then_inc(wt_ps, 1)

        @block.scalar
        def _(act):
            for t in range(TT):
                act.wait_ge(x1_done, t + 1)
                nc.scalar.activation(sqs, x1[:, t, :], ACT.Square, accum_out=ss[:, t:t + 1])
                nc.scalar.drain()
            nc.scalar.drain().then_inc(ss_done, 1)
            act.wait_ge(rt, 1)
            nc.scalar.activation(rstd, rstd, ACT.Sqrt)
            nc.scalar.drain().then_inc(ss_done, 1)
            for g in range(TT * 2):
                t, half = divmod(g, 2)
                act.wait_ge(ht_ps, g + 1)
                nc.scalar.activation(h2T[:, half * 4:half * 4 + 4, t * P:(t + 1) * P], heads(PS[:, g % 4, :]), ACT.Copy).then_inc(ht_sb, 1)
            act.wait_ge(lg_ready, 1)
            nc.scalar.activation(aff, aff, ACT.Exp).then_inc(aff_e, 1)
            for i in range(NE // 2):
                act.wait_ge(wt_ps, i + 1)
                nc.scalar.activation(WTp[:, i, :], PS[:, i % 4, :], ACT.Copy).then_inc(wt_sb, 1)

        @block.vector
        def _(dve):
            dve.wait_ge(x_in2, 16)
            for g in range(TT * 2):
                hf, t = divmod(g, TT)
                dve.wait_ge(y_ps, g + 1)
                x = x1[:, t, hf * 512:(hf + 1) * 512]
                nc.vector.tensor_tensor(tmp[:, g % 2, :], PS[:, g, :], GT1[:, hf * 512:(hf + 1) * 512], ALU.mult)
                nc.vector.drain()
                nc.vector.tensor_tensor(x, x, tmp[:, g % 2, :], ALU.add)
                if hf == 1:
                    nc.vector.drain().then_inc(x1_done, 1)
            dve.wait_ge(ss_done, 1)
            nc.vector.tensor_scalar(rstd, ss, 1.0 / D, EPS, ALU.mult, ALU.add).then_inc(rt, 1)
            dve.wait_ge(ss_done, 2)
            nc.vector.reciprocal(rstd, rstd)
            nc.vector.drain()
            for t in range(TT):
                nc.vector.scalar_tensor_tensor(h2[:, t, :], x1[:, t, :], rstd[:, t:t + 1], A2, ALU.mult, ALU.mult)
                nc.vector.drain()
                nc.vector.tensor_tensor(h2[:, t, :], h2[:, t, :], SH2, ALU.add).then_inc(h2_done, 1)
            dve.wait_ge(lg_ps, 1)
            lg = PS[:, 4, 0:NE * TT].rearrange("p (t e) -> p t e", t=TT)
            nc.vector.reduce_max(m4, lg, AX.X)
            nc.vector.drain()
            nc.vector.tensor_tensor(aff, lg, spread(m4, NE), ALU.subtract).then_inc(lg_ready, 1)
            dve.wait_ge(aff_e, 1)
            nc.vector.reduce_sum(m4, aff, AX.X)
            nc.vector.drain()
            nc.vector.reciprocal(m4, m4)
            nc.vector.drain()
            nc.vector.tensor_tensor(aff, aff, spread(m4, NE), ALU.mult).then_inc(aff_done, 1)
            dve.wait_ge(aft_ps, 1)
            nc.vector.tensor_copy(work[0:NE, :], PS[0:NE, 5, :])
            for r in range(CAP // 8):
                nc.vector.drain()
                nc.vector.max(top8[0:NE, :], work[0:NE, :])
                nc.vector.drain()
                nc.vector.match_replace(out=work[0:NE, :], in_to_replace=top8[0:NE, :], in_values=work[0:NE, :], imm_value=-1.0)
            nc.vector.drain()
            nc.vector.tensor_scalar(work[0:NE, :], work[0:NE, :], 0.0, None, ALU.is_lt)
            nc.vector.memset(affT[0:NE, :], 1.0)
            nc.vector.drain()
            nc.vector.tensor_tensor_scan(affT[0:NE, :], work[0:NE, :], affT[0:NE, :], 0.0, ALU.add, ALU.mult)
            nc.vector.drain()
            nc.vector.tensor_tensor(work[0:NE, :], work[0:NE, :], affT[0:NE, :], ALU.mult)
            nc.vector.drain()
            dve.wait_ge(code_zero, 1)
            nc.vector.tensor_scalar(code[0:NE, :], work[0:NE, :], -1.0, None, ALU.add).then_inc(code_done, 1)
            dve.wait_ge(ct_ps, 1)
            nc.vector.tensor_copy(codet, PS[:, 6, :].rearrange("p (t e) -> p t e", t=TT)[:, :, 0:NE])
            nc.vector.drain()
            for t in range(TT):
                nc.vector.tensor_tensor(heads(onehot[:, t, :], NE), over(C["iota"], NE), spread(codet[:, t, :], CAP),
                                        ALU.is_equal).then_inc(oh_sb, 1)

    base = [W1N // RING1] * RING1 + [0] * (RING - RING1)
    xe_ps, xe_sb, gu_ps, hs_sb, hid_sb, hd_ps, hd_v, hd_a, ye_ps, ye_sb, cb_ps, cb_sb, wc_sb = (sem(x) for x in (
        "xe_ps", "xe_sb", "gu_ps", "hs_sb", "hid_sb", "hd_ps", "hd_v", "hd_a", "ye_ps", "ye_sb", "cb_ps", "cb_sb", "wc_sb"))
    NP = NE // 2
    LO, HI = (0, CAP), (CAP, 2 * CAP)
    GATE, UP = [HI, LO], [LO, HI]
    OWN = [LO, HI]
    with nc.Block("experts") as block:
        @block.sync
        def _(sp):
            for s in range(RING1, RING):
                load_expert_chunk(sp, 0, s)
            with sp.Fori(1, NE) as n:
                for s in range(RING):
                    sp.wait_ge(used, RING * n + (W1N - RING + 1 + s))
                    load_expert_chunk(sp, n, s)
            for s in range(RING):
                sp.wait_ge(used, W1N + WEN - RING + 1 + s)
                sp.dma_start(slots[s], A["wts"][W1N + WEN + s, :, :]).then_inc(arrived[s], 16)

        @block.tensor
        def _(pe):
            with pe.Fori(0, NP) as i:
                def chunk(c):
                    s = c % RING
                    pe.wait_ge(arrived[s], 32 * i + 16 * (base[s] + c // RING + 1))
                    return slots[s].rearrange("p (k n) -> p k n", k=DK)

                for k in range(DK):
                    for t in range(TT):
                        last = nc.tensor.matmul(PS[:, k // 4, (k % 4) * P:(k % 4 + 1) * P], h2[:, t, k * P:(k + 1) * P],
                                                onehot[:, t, bass.ds(2 * CAP * i, 2 * CAP)], start=(t == 0), stop=(t == TT - 1))
                last.then_inc(xe_ps, 1)
                pe.wait_ge(xe_sb, i + 1)
                for j in range(2):
                    for half in range(2):
                        g, u = chunk(4 * j + 2 * half), chunk(4 * j + 2 * half + 1)
                        for k in range(DK):
                            for w, (a, b) in ((g, GATE[j]), (u, UP[j])):
                                last = nc.tensor.matmul(PS[a:b, 2 + 2 * j + half, :], xe[:, k, j * CAP:(j + 1) * CAP], w[:, k, :],
                                                        start=(k == 0), stop=(k == DK - 1))
                        last.then_inc(gu_ps, 1)
                        nc.tensor.drain().then_inc(used, 2)
                for half in range(2):
                    pe.wait_ge(hid_sb, 4 * i + (3 + half))
                    for f in range(4):
                        c = half * 512 + f * P
                        last = nc.tensor.transpose(PS[:, 6 + half, f * P:(f + 1) * P], hid[:, c:c + P], C["ident"])
                    last.then_inc(hd_ps, 1)
                for half in range(2):
                    w = [chunk(8 + 2 * half), chunk(9 + 2 * half)]
                    for k in range(DK):
                        if half == 0 and k % 4 == 0:
                            pe.wait_ge(hd_a if k else hd_v, i + 1)
                        for j, (a, b) in enumerate(OWN):
                            last = nc.tensor.matmul(PS[a:b, 2 + half, :], hidT[:, k, j * CAP:(j + 1) * CAP], w[j][:, k, :],
                                                    start=(k == 0), stop=(k == DK - 1))
                    last.then_inc(ye_ps, 1)
                    nc.tensor.drain().then_inc(used, 2)
                pe.wait_ge(wc_sb, i + 1)
                pe.wait_ge(ye_sb, 2 * i + 2)
                for c in range(2 * TT):
                    t, half = divmod(c, 2)
                    pe.wait_ge(cb_sb, 8 * i + (c + 1))
                    nc.tensor.matmul(PS[:, 4 + c % 2, :], wcur[:, t * P:(t + 1) * P], ye[:, half * 512:(half + 1) * 512],
                                     start=True, stop=True).then_inc(cb_ps, 1)

        @block.scalar
        def _(act):
            with act.Fori(0, NP) as i:
                for j in range(2):
                    (a, b), (c, d) = GATE[j], OWN[j]
                    for half in range(2):
                        act.wait_ge(gu_ps, 4 * i + (2 * j + half + 1))
                        nc.scalar.activation(hs[c:d, half * 512:(half + 1) * 512], PS[a:b, 2 + 2 * j + half, :],
                                             ACT.Silu).then_inc(hs_sb, 1)
                act.wait_ge(hd_ps, 2 * i + 2)
                nc.scalar.activation(hidT[:, 4:8, :].rearrange("p k n -> p (k n)"), PS[:, 7, :], ACT.Copy).then_inc(hd_a, 1)

        @block.vector
        def _(dve):
            nc.vector.drain().then_inc(cb_sb, 2)
            with dve.Fori(0, NP) as i:
                dve.wait_ge(xe_ps, i + 1)
                nc.vector.tensor_copy(xe.rearrange("p k n -> p (k n)").rearrange("p (a n) -> p a n", a=2), PS[:, 0:2, :]).then_inc(xe_sb, 1)
                nc.vector.tensor_copy(wcur, WTp[:, bass.ds(i, 1), :].rearrange("p a n -> p (a n)")).then_inc(wc_sb, 1)
                for j in range(2):
                    (a, b) = OWN[j]
                    for half in range(2):
                        lo, hi = half * 512, (half + 1) * 512
                        dve.wait_ge(hs_sb, 4 * i + (2 * j + half + 1))
                        nc.vector.tensor_tensor(hid[a:b, lo:hi], hs[a:b, lo:hi], PS[a:b, 2 + 2 * j + half, :], ALU.mult).then_inc(hid_sb, 1)
                dve.wait_ge(hd_ps, 2 * i + 1)
                nc.vector.tensor_copy(hidT[:, 0:4, :].rearrange("p k n -> p (k n)"), PS[:, 6, :]).then_inc(hd_v, 1)
                for half in range(2):
                    dve.wait_ge(ye_ps, 2 * i + (half + 1))
                    lo, hi = half * 512, (half + 1) * 512
                    nc.vector.tensor_tensor(ye[:, lo:hi], PS[:, 2 + half, :], GT2[:, lo:hi], ALU.mult).then_inc(ye_sb, 1)
                for c in range(2 * TT):
                    t, half = divmod(c, 2)
                    dve.wait_ge(cb_ps, 8 * i + (c + 1))
                    x = x1[:, t, half * 512:(half + 1) * 512]
                    nc.vector.tensor_tensor(x, x, PS[:, 4 + c % 2, :], ALU.add).then_inc(cb_sb, 1)

    fn_in, fss, frt, frs, fx = (sem(x) for x in ("fn_in", "fss", "frt", "frs", "fx"))
    fnw, sq2 = h2[:, 0, :], h2[:, 1, :]
    with nc.Block("first_norm") as block:
        @block.scalar
        def _(act):
            act.dma_start(fnw, A["final_norm"].partition_broadcast(P)).then_inc(fn_in, 16)
            for t in range(TT):
                nc.scalar.activation(sq2, x1[:, t, :], ACT.Square, accum_out=ss[:, t:t + 1])
                nc.scalar.drain()
            nc.scalar.drain().then_inc(fss, 1)
            act.wait_ge(frs, 1)
            nc.scalar.activation(rstd, rstd, ACT.Sqrt).then_inc(frt, 1)

        @block.vector
        def _(dve):
            dve.wait_ge(fss, 1)
            nc.vector.tensor_scalar(rstd, ss, 1.0 / D, EPS, ALU.mult, ALU.add).then_inc(frs, 1)
            dve.wait_ge(frt, 1)
            dve.wait_ge(fn_in, 16)
            nc.vector.reciprocal(rstd, rstd)
            nc.vector.drain()
            for t in range(TT):
                nc.vector.scalar_tensor_tensor(x1[:, t, :], x1[:, t, :], rstd[:, t:t + 1], fnw, ALU.mult, ALU.mult)
    E["x1"], E["rest_at"] = x1, V["rest_at"]
    sem.close()


W13SZ, W2SZ = SLOT, FT * P
CSIZE = ([W13SZ] * W13C + [W2SZ] * W2C + [4 * D, 2 * D, 4 * D, 4 * D, 4 * D, SLOT] + [2 * D] * 4 +
         [W13SZ] * W13C + [W2SZ] * W2C)
C_MIX, C_OUT, C_FFN2 = W13C + W2C, W13C + W2C + 6, W13C + W2C + 10
assert len(CSIZE) == LAYC
PARS, NPAR = offsets({k: np.zeros((1, n)) for k, n in [
    ("ln_g", 24), ("ln_b", 24), ("pool_scale", 2), ("conv_db", 2), ("conv_g", 2), ("conv_b", 2), ("gn", 4), ("dw", 2 * CW),
    ("pool_w", 2 * P), ("pw", 2 * 256)]})


def second_block(E):
    nc, A, arena, PS, slots = (E[k] for k in ("nc", "A", "arena", "PS", "slots"))
    used, arrived, x1 = E["used"], E["arrived"], E["x1"]
    sem = E["sem"]
    o2, n2 = offsets(table2())
    B = Map(arena, RING * SLOT, E["TOTAL"])
    tab = B.take(n2)
    C = {k: tab[:, a:a + n] for k, (a, n) in o2.items()}
    res = B.take(DK, L)
    hT = B.take(DK, L)
    gT_at = B.at
    gT = B.take(FT, L)
    par = B.take(NPAR)
    pr = {k: par[:, a:a + n] for k, (a, n) in PARS.items()}
    lnin = B.take(2 * DK)
    free_at = B.at
    M = Map(arena, gT_at, gT_at + FT * L)
    sqT = M.take(DK, L)
    rs = M.take(L)
    res_at = RING * SLOT + n2
    M = Map(arena, gT_at, gT_at + FT * L)
    qT, kT, sg, v = M.take(RH, L), M.take(RH, L), M.take(RH, L), M.take(5, 512)
    u, acc = M.take(2, CW - 1 + L), M.take(2, L)
    M2 = Map(arena, free_at, E["TOTAL"])
    yp = M2.take(2, L)
    M3 = Map(arena, res_at, res_at + DK * L)
    sT = M3.take(1808)
    xp, win2 = M3.take(2, 544), M3.take(2, 544)
    ropet = sT[:, 0:2 * L].rearrange("p (a n) -> p a n", a=2)
    M4 = Map(arena, M.at, gT_at + FT * L)
    mrs = M4.take(L)
    M5 = Map(arena, M2.at, E["TOTAL"])
    msq = M5.take(L)
    msq2 = M4.take(L) if M4.at + L <= M4.end else M5.take(L)
    sq2 = [msq, msq2]

    def halves(ap):
        return ap.rearrange("p (a n) -> p a n", a=2)

    def bank(b, h=None):
        return PS[:, b:b + 2, 0:LH] if h is None else PS[:, b + h, 0:LH]

    in_ld, it_ps, it_a, it_v = sem("in_ld"), sem("it_ps"), sem("it_a"), sem("it_v")
    with nc.Block("to_features") as block:
        @block.sync
        def _(sp):
            sp.dma_start(tab, A["tab2"]).then_inc(in_ld, 16)
            sp.dma_start(lnin, A["ln_in"]).then_inc(in_ld, 16)
            sp.dma_start(res[:, :, 0:NMETA], A["meta"].rearrange("p (k n) -> p k n", k=DK)).then_inc(in_ld, 16)

        @block.tensor
        def _(pe):
            pe.wait_ge(in_ld, 48)
            for g in range(2 * TT):
                t, half = divmod(g, 2)
                for i in range(4):
                    k = half * 4 + i
                    last = nc.tensor.transpose(PS[:, g, i * P:(i + 1) * P], x1[:, t, k * P:(k + 1) * P], C["ident"])
                last.then_inc(it_ps, 1)

        @block.scalar
        def _(act):
            for g in range(0, 2 * TT, 2):
                act.wait_ge(it_ps, g + 1)
                t = g // 2
                nc.scalar.activation(res[:, 0:4, NMETA + t * P:NMETA + (t + 1) * P], heads(PS[:, g, :]), ACT.Copy)

        @block.vector
        def _(dve):
            for g in range(1, 2 * TT, 2):
                dve.wait_ge(it_ps, g + 1)
                t = g // 2
                nc.vector.tensor_copy(res[:, 4:8, NMETA + t * P:NMETA + (t + 1) * P], heads(PS[:, g, :]))

    class Sig:

        def __init__(self, name, per, first=0):
            self.sem, self.per, self.first = sem(name), per, first

        def wait(self, eng, l, n):
            eng.wait_ge(self.sem, n if l is None else l * self.per + (self.first + n))

    ln_m, ln_v, ln_e, ln_r = (Sig(x, 3, 1) for x in ("ln_m", "ln_v", "ln_e", "ln_r"))
    ln_c, ln_q, ln_n, ln_h = (Sig(x, 3 * DK, DK) for x in ("ln_c", "ln_q", "ln_n", "ln_h"))

    def ln_pe(pe, l, uu, ready):
        for k in range(DK):
            ready(pe, k)
            for h in range(2):
                last = nc.tensor.matmul(bank(0, h), C["mean_d"], halves(res[:, k, :])[:, h, :], start=(k == 0), stop=(k == DK - 1))
        last.then_inc(ln_m.sem, 1)
        for k in range(DK):
            ln_q.wait(pe, l, uu * DK + k + 1)
            for h in range(2):
                last = nc.tensor.matmul(bank(2, h), C["mean_d"], halves(sqT[:, k, :])[:, h, :], start=(k == 0), stop=(k == DK - 1))
        last.then_inc(ln_v.sem, 1)

    def ln_dve(dve, l, uu):
        ln_m.wait(dve, l, uu + 1)
        for k in range(DK):
            nc.vector.tensor_tensor(halves(res[:, k, :]), halves(res[:, k, :]), bank(0), ALU.subtract).then_inc(ln_c.sem, 1)
        ln_v.wait(dve, l, uu + 1)
        nc.vector.tensor_scalar(halves(rs), bank(2), LN_EPS, None, ALU.add).then_inc(ln_e.sem, 1)
        ln_r.wait(dve, l, uu + 1)
        nc.vector.reciprocal(rs, rs)
        nc.vector.drain()
        for k in range(DK):
            nc.vector.tensor_tensor(res[:, k, :], res[:, k, :], rs, ALU.mult).then_inc(ln_n.sem, 1)

    def ln_act(act, l, uu, gain, shift):
        for k in range(DK):
            ln_c.wait(act, l, uu * DK + k + 1)
            nc.scalar.activation(sqT[:, k, :], res[:, k, :], ACT.Square).then_inc(ln_q.sem, 1)
        ln_e.wait(act, l, uu + 1)
        nc.scalar.activation(rs, rs, ACT.Sqrt).then_inc(ln_r.sem, 1)
        for k in range(DK):
            ln_n.wait(act, l, uu * DK + k + 1)
            nc.scalar.activation(hT[:, k, :], res[:, k, :], ACT.Identity, scale=gain[:, k:k + 1], bias=shift[:, k:k + 1]).then_inc(ln_h.sem, 1)

    up_ps, sl_sb, g_sb = Sig("up_ps", 4 * FT), Sig("sl_sb", 2 * FT), Sig("g_sb", 2 * FT)
    dn_ps, ah_sb, dn_sb = (Sig(x, 2 * DK) for x in ("dn_ps", "ah_sb", "dn_sb"))
    base = [W1N // RING1 + NE] * RING1 + [NE] * (RING - RING1)

    def chunk(pe, l, c):
        s = c % RING
        pe.wait_ge(arrived[s], l * (16 * LAYC // RING) + 16 * (base[s] + c // RING + 1))
        return slots[s]

    def release(pe):
        nc.tensor.drain().then_inc(used, 1)

    def ffn_pe(pe, l, w):
        c0 = w * C_FFN2
        for f in range(FT):
            if f % 2 == 0:
                wt = chunk(pe, l, c0 + f // 2).rearrange("p (f z k n) -> p f z k n", f=2, z=2, k=DK)
            for z in range(2):
                if f >= 2:
                    (g_sb if z else sl_sb).wait(pe, l, w * FT + f - 1)
                for k in range(DK):
                    if f == 0 and z == 0:
                        ln_h.wait(pe, l, 2 * w * DK + k + 1 - DK)
                    for h in range(2):
                        last = nc.tensor.matmul(bank(4 * (f % 2) + 2 * z, h), wt[:, f % 2, z, k, :], halves(hT[:, k, :])[:, h, :],
                                                start=(k == 0), stop=(k == DK - 1))
                last.then_inc(up_ps.sem, 1)
            if f % 2:
                release(pe)
        for m in range(DK):
            wt = chunk(pe, l, c0 + W13C + m)[:, 0:FT * P].rearrange("p (f n) -> p f n", f=FT)
            if m >= 4:
                dn_sb.wait(pe, l, w * DK + m - 3)
            for f in range(FT):
                if m == 0 and f in (0, FT - 2, FT - 1):
                    g_sb.wait(pe, l, w * FT + max(f + 1, FT - 2))
                if m == 0 and f == 0:
                    sl_sb.wait(pe, l, w * FT + FT - 1)
                if m == 2 and f == 0:
                    sl_sb.wait(pe, l, w * FT + FT)
                if m == 1 and f == 0:
                    g_sb.wait(pe, l, w * FT + FT)
                for h in range(2):
                    last = nc.tensor.matmul(bank(2 * (m % 4), h), wt[:, f, :], halves(gT[:, f, :])[:, h, :],
                                            start=(f == 0), stop=(f == FT - 1))
            last.then_inc(dn_ps.sem, 1)
            release(pe)

    def ffn_act(act, l, w):
        nc.scalar.drain()
        for k in range(DK):
            nc.scalar.activation(res[:, k, :], hT[:, k, :], ACT.Copy, scale=ALPHA).then_inc(ah_sb.sem, 1)
        for f in range(FT):
            up_ps.wait(act, l, 2 * (w * FT + f) + 1)
            nc.scalar.activation(halves(gT[:, f, :]), bank(4 * (f % 2)), ACT.Silu).then_inc(sl_sb.sem, 1)

    def ffn_dve(dve, l, w):
        for f in range(FT):
            up_ps.wait(dve, l, 2 * (w * FT + f) + 2)
            sl_sb.wait(dve, l, w * FT + f + 1)
            nc.vector.tensor_tensor(halves(gT[:, f, :]), halves(gT[:, f, :]), bank(4 * (f % 2) + 2), ALU.mult).then_inc(g_sb.sem, 1)
        for m in range(DK):
            ah_sb.wait(dve, l, w * DK + m + 1)
            dn_ps.wait(dve, l, w * DK + m + 1)
            nc.vector.scalar_tensor_tensor(halves(res[:, m, :]), bank(2 * (m % 4)), 0.5, halves(res[:, m, :]),
                                           ALU.mult, ALU.add).then_inc(dn_sb.sem, 1)

    units = ([("xp", t, "a") for t in range(2)] + [("ca", t, "v") for t in range(2)] + [("cg", t, "a") for t in range(2)] +
             [("q", t, "v") for t in range(4)] + [("k", t, "v") for t in range(4)] + [("g", t, "a") for t in range(4)] +
             [("v", t, "a") for t in range(5)] + [("pool", t, "a") for t in range(2)])
    count = {"a": 0, "v": 0}
    done = []
    for _, _, e in units:
        count[e] += 1
        done.append((e, count[e]))
    NU = len(units)
    u_ps, u_a, u_v = Sig("u_ps", NU), Sig("u_a", count["a"]), Sig("u_v", count["v"])
    rope_s, kq_sb, yp_sb, cv_sb = Sig("rope_s", 8), Sig("kq_sb", 8), Sig("yp_sb", 2), Sig("cv_sb", 2)
    cm_ps, cc_sb, cq_sb, cvar, ce, cr, cn_sb, cs_sb, pw_ps, pw_sb = (Sig(x, n) for x, n in (
        ("cm_ps", 1), ("cc_sb", 2), ("cq_sb", 2), ("cvar", 1), ("ce", 1), ("cr", 1), ("cn_sb", 2), ("cs_sb", 2), ("pw_ps", 2), ("pw_sb", 2)))
    st_ps, st_sb, ro_ps, ro_sb = (Sig(x, RH) for x in ("st_ps", "st_sb", "ro_ps", "ro_sb"))
    gm_ps, gc_sb, gq_sb, gv_ps, ge, gr, gy_sb = (Sig(x, RH) for x in ("gm_ps", "gc_sb", "gq_sb", "gv_ps", "ge", "gr", "gy_sb"))
    wo_ps, wo_sb = Sig("wo_ps", DK), Sig("wo_sb", DK)
    xz_sb = Sig("xz_sb", 1)
    par_in = Sig("par_in", 16)
    KCOL = [0, L, L + T, L + T + 384, L + T + 384 + 256]
    KWID = [L] + [T - P * i for i in range(TT)]
    KBANK = [(0, 0), (2, 0), (3, 0), (4, 0), (4, 256)]
    ymix = [yp[:, 0, :], yp[:, 1, :], u[:, 0, 0:L], u[:, 1, 0:L]] + [qT[:, h, :] for h in range(RH)]

    def mix_pe(pe, l):
        def free(w):
            if w >= 4:
                e, n = done[w - 4]
                (u_a if e == "a" else u_v).wait(pe, l, n)
        for w, (kind, t, _) in enumerate(units):
            free(w)
            if kind == "pool":
                yp_sb.wait(pe, l, t + 1)
                for h in range(2):
                    last = nc.tensor.matmul(bank(2 * (w % 4), h), pr["pool_w"][:, t * P:(t + 1) * P], halves(yp[:, t, :])[:, h, :],
                                            start=True, stop=True)
                last.then_inc(u_ps.sem, 1)
                continue
            j = {"xp": 0, "ca": 0, "cg": 1, "q": 2, "k": 3, "g": 4, "v": 5}[kind]
            if t == 0 and kind != "ca":
                wt = chunk(pe, l, C_MIX + j)
            if kind == "v":
                s, n = TILES[t]
                wv = wt.rearrange("p (k n) -> p k n", k=DK)
                for k in range(DK):
                    last = nc.tensor.matmul(PS[0:n, 2 * (w % 4), :], hT[:, k, s:s + n], wv[:, k, :], start=(k == 0), stop=(k == DK - 1))
            else:
                at = (t + (2 if kind == "ca" else 0)) * D
                wv = wt[:, at:at + D].rearrange("p (k n) -> p k n", k=DK)
                for k in range(DK):
                    if w == 0:
                        ln_h.wait(pe, l, k + 1)
                    for h in range(2):
                        last = nc.tensor.matmul(bank(2 * (w % 4), h), wv[:, k, :], halves(hT[:, k, :])[:, h, :],
                                                start=(k == 0), stop=(k == DK - 1))
            last.then_inc(u_ps.sem, 1)
            if (kind, t) in (("ca", 1), ("cg", 1), ("q", 3), ("k", 3), ("g", 3), ("v", 4)):
                release(pe)
        u_a.wait(pe, l, count["a"])
        for t in range(2):
            cv_sb.wait(pe, l, t + 1)
            for h in range(2):
                last = nc.tensor.matmul(bank(0, h), C["mean_c"], halves(acc[:, t, :])[:, h, :], start=(t == 0), stop=(t == 1))
        last.then_inc(cm_ps.sem, 1)
        for t in range(2):
            cq_sb.wait(pe, l, t + 1)
            for h in range(2):
                last = nc.tensor.matmul(bank(2, h), C["mean_c"], halves(sq2[t])[:, h, :], start=(t == 0), stop=(t == 1))
        last.then_inc(cvar.sem, 1)
        pw = pr["pw"].rearrange("p (k n) -> p k n", k=2)
        for m in range(2):
            for t in range(2):
                cs_sb.wait(pe, l, t + 1)
                for h in range(2):
                    last = nc.tensor.matmul(bank(4 + 2 * m, h), pw[:, t, m * P:(m + 1) * P], halves(acc[:, t, :])[:, h, :],
                                            start=(t == 0), stop=(t == 1))
            last.then_inc(pw_ps.sem, 1)
        pw_sb.wait(pe, l, 2)
        for h in range(RH):
            kq_sb.wait(pe, l, 5 + h)
            if h == 0:
                ce.wait(pe, l, 1)
            else:
                st_sb.wait(pe, l, h)
            for i, (s, n) in enumerate(TILES):
                b, c = KBANK[i]
                if i == 0:
                    for hf in range(2):
                        nc.tensor.matmul(PS[0:n, hf, 0:LH], kT[:, h, s:s + n], halves(qT[:, h, :])[:, hf, :], start=True, stop=True)
                else:
                    last = nc.tensor.matmul(PS[:, b, c:c + KWID[i]], kT[:, h, s:s + n], qT[:, h, s:], start=True, stop=True)
            last.then_inc(st_ps.sem, 1)
            st_sb.wait(pe, l, h + 1)
            if h:
                ro_sb.wait(pe, l, h)
            for hf in range(2):
                lo, hi = hf * LH, (hf + 1) * LH
                parts = [i for i, (s, n) in enumerate(TILES) if s < hi]
                for i in parts:
                    s, n = TILES[i]
                    a = max(s, lo) if i else lo
                    c = KCOL[i] + a - (s if i else 0)
                    last = nc.tensor.matmul(PS[:, 5 + hf, a - lo:LH], v[0:n, i, h * P:(h + 1) * P], sT[0:n, c:c + hi - a],
                                            start=(i == 0), stop=(i == parts[-1]))
            last.then_inc(ro_ps.sem, 1)
        for h in range(RH):
            ro_sb.wait(pe, l, RH if h else RH)
            b = 4 * (h % 2)
            if h >= 2:
                ge.wait(pe, l, h - 1)
            for hf in range(2):
                last = nc.tensor.matmul(bank(b, hf), C["mean_h"], halves(qT[:, h, :])[:, hf, :], start=True, stop=True)
            last.then_inc(gm_ps.sem, 1)
            gq_sb.wait(pe, l, h + 1)
            for hf in range(2):
                last = nc.tensor.matmul(bank(b + 2, hf), C["mean_h"], halves(sq2[h % 2])[:, hf, :], start=True, stop=True)
            last.then_inc(gv_ps.sem, 1)
        ge.wait(pe, l, RH)
        for m in range(DK):
            if m % 2 == 0:
                wt = chunk(pe, l, C_OUT + m // 2)[:, 0:2 * D].rearrange("p (m k n) -> p m k n", m=2, k=DK)
            if m >= 4:
                wo_sb.wait(pe, l, m - 3)
            for k in range(DK):
                if m == 0 and k >= 4:
                    gy_sb.wait(pe, l, k - 3)
                for h in range(2):
                    last = nc.tensor.matmul(bank(2 * (m % 4), h), wt[:, m % 2, k, :], halves(ymix[k])[:, h, :], start=(k == 0), stop=(k == DK - 1))
            last.then_inc(wo_ps.sem, 1)
            if m % 2:
                release(pe)

    def mix_act(act, l):
        xz_sb.wait(act, l, 1)
        for w, (kind, t, e) in enumerate(units):
            if e != "a":
                continue
            b = 2 * (w % 4)
            u_ps.wait(act, l, w + 1)
            if kind == "xp":
                nc.scalar.activation(halves(xp[:, t, 16:]), bank(b), ACT.Copy).then_inc(u_a.sem, 1)
            elif kind == "cg":
                nc.scalar.activation(halves(acc[:, t, :]), bank(b), ACT.Sigmoid).then_inc(u_a.sem, 1)
            elif kind == "g":
                nc.scalar.activation(halves(sg[:, t, :]), bank(b), ACT.Silu).then_inc(u_a.sem, 1)
            elif kind == "v":
                n = TILES[t][1]
                nc.scalar.activation(v[0:n, t, :], PS[0:n, b, :], ACT.Copy).then_inc(u_a.sem, 1)
            else:
                nc.scalar.activation(halves(yp[:, t, :]), bank(b), ACT.Copy, scale=pr["pool_scale"][:, t:t + 1]).then_inc(u_a.sem, 1)
        for t in range(2):
            cc_sb.wait(act, l, t + 1)
            nc.scalar.activation(sq2[t], acc[:, t, :], ACT.Square).then_inc(cq_sb.sem, 1)
        ce.wait(act, l, 1)
        nc.scalar.activation(mrs, mrs, ACT.Sqrt).then_inc(cr.sem, 1)
        for t in range(2):
            cn_sb.wait(act, l, t + 1)
            nc.scalar.activation(acc[:, t, :], acc[:, t, :], ACT.Silu, scale=pr["conv_g"][:, t:t + 1], bias=pr["conv_b"][:, t:t + 1]).then_inc(cs_sb.sem, 1)
        for t in range(2):
            pw_ps.wait(act, l, t + 1)
            nc.scalar.activation(halves(u[:, t, 0:L]), bank(4 + 2 * t), ACT.Copy).then_inc(pw_sb.sem, 1)
        for h in range(RH):
            ro_ps.wait(act, l, h + 1)
            nc.scalar.activation(halves(qT[:, h, :]), bank(5), ACT.Copy).then_inc(ro_sb.sem, 1)
        for h in range(RH):
            gc_sb.wait(act, l, h + 1)
            nc.scalar.activation(sq2[h % 2], qT[:, h, :], ACT.Square).then_inc(gq_sb.sem, 1)
            ge.wait(act, l, h + 1)
            nc.scalar.activation(mrs, mrs, ACT.Sqrt).then_inc(gr.sem, 1)

    def mix_pool(pool, l):
        if True:
            ln_h.wait(pool, l, DK)
            nc.gpsimd.tensor_tensor(xp[:, 0, 0:16], C["cnt"][:, 0:16], C["cnt"][:, 0:16], ALU.subtract)
            nc.gpsimd.memset(xp[:, 1, 0:16], 0.0)
            nc.gpsimd.memset(u[:, :, 0:CW - 1], 0.0)
            nc.gpsimd.drain().then_inc(xz_sb.sem, 1)
        for t in range(2):
            u_a.wait(pool, l, t + 1)
            x, s, r = xp[:, t, :], win2[:, 0, :], win2[:, 1, :]
            src, sh, dst = x, 1, s
            for step in range(2 if t == 0 else 4):
                nc.gpsimd.tensor_tensor(dst[:, 2 * sh:], src[:, 2 * sh:], src[:, sh:544 - sh], ALU.add)
                nc.gpsimd.drain()
                src, sh, dst = dst, 2 * sh, (r if dst is s else s)
            for half, y in ((0, s), (1, r)):
                a, b = half * 64, half * 64 + 64
                nc.gpsimd.tensor_tensor(yp[a:b, t, 0:16], y[a:b, 16:32], C["cnt"][a:b, 16 * t:16 * t + 16], ALU.mult)
                nc.gpsimd.tensor_scalar(yp[a:b, t, 16:], y[a:b, 32:544], C["win"][a:b, t:t + 1], None, ALU.mult)
            nc.gpsimd.drain()
            nc.gpsimd.tensor_tensor(yp[:, t, :], yp[:, t, :], x[:, 16:544], ALU.subtract)
            nc.gpsimd.drain().then_inc(yp_sb.sem, 1)
        for i in range(8):
            rope_s.wait(pool, l, i + 1)
            x = (qT if i < 4 else kT)[:, i % 4, :]
            nc.gpsimd.tensor_tensor(x, x, ropet[:, i % 2, :], ALU.add).then_inc(kq_sb.sem, 1)

    def mix_dve(dve, l):
        for t in range(2):
            u_a.wait(dve, l, 3 + t)
            nc.vector.tensor_tensor(halves(u[:, t, CW - 1:]), halves(acc[:, t, :]), bank(2 * ((2 + t) % 4)), ALU.mult).then_inc(u_v.sem, 1)
        for i in range(8):
            w = 6 + i
            b = 2 * (w % 4)
            u_ps.wait(dve, l, w + 1)
            if i >= 2:
                kq_sb.wait(dve, l, i - 1)
            x = (qT if i < 4 else kT)[:, i % 4, :]
            nc.vector.tensor_tensor(halves(x), bank(b), halves(C["cos"]), ALU.mult)
            nc.vector.tensor_tensor(halves(ropet[0:64, i % 2, :]), PS[64:128, b:b + 2, 0:LH], halves(C["sin"][64:128, :]), ALU.mult)
            nc.vector.tensor_tensor(halves(ropet[64:128, i % 2, :]), PS[0:64, b:b + 2, 0:LH], halves(C["sin"][0:64, :]), ALU.mult)
            nc.vector.drain().then_inc(rope_s.sem, 1)
            nc.vector.drain().then_inc(u_v.sem, 1)
        par_in.wait(dve, l, 16)
        xz_sb.wait(dve, l, 1)
        for w in range(CW):
            for t in range(2):
                k = pr["dw"][:, t * CW + w:t * CW + w + 1]
                if w == 0:
                    last = nc.vector.tensor_scalar(acc[:, t, :], u[:, t, w:w + L], k, pr["conv_db"][:, t:t + 1], ALU.mult, ALU.add)
                else:
                    last = nc.vector.scalar_tensor_tensor(acc[:, t, :], u[:, t, w:w + L], k, acc[:, t, :], ALU.mult, ALU.add)
                if w == CW - 1:
                    last.then_inc(cv_sb.sem, 1)
            nc.vector.drain()
        cm_ps.wait(dve, l, 1)
        for t in range(2):
            nc.vector.tensor_tensor(halves(acc[:, t, :]), halves(acc[:, t, :]), bank(0), ALU.subtract).then_inc(cc_sb.sem, 1)
        cvar.wait(dve, l, 1)
        nc.vector.tensor_scalar(halves(mrs), bank(2), LN_EPS, None, ALU.add).then_inc(ce.sem, 1)
        cr.wait(dve, l, 1)
        nc.vector.reciprocal(mrs, mrs)
        nc.vector.drain()
        for t in range(2):
            nc.vector.tensor_tensor(acc[:, t, :], acc[:, t, :], mrs, ALU.mult).then_inc(cn_sb.sem, 1)
        kq_sb.wait(dve, l, 8)
        for h in range(RH):
            st_ps.wait(dve, l, h + 1)
            if h:
                ro_ps.wait(dve, l, h)
            dc = C["decay"][:, h * L:(h + 1) * L]
            nc.vector.tensor_tensor(halves(sT[0:NMETA, 0:L]), PS[0:NMETA, 0:2, 0:LH], halves(dc[0:NMETA, :]), ALU.mult)
            for i in range(1, 5):
                b, c = KBANK[i]
                nc.vector.tensor_tensor(sT[:, KCOL[i]:KCOL[i] + KWID[i]], PS[:, b, c:c + KWID[i]], dc[:, 0:KWID[i]], ALU.mult)
            nc.vector.drain().then_inc(st_sb.sem, 1)
        for h in range(RH):
            b = 4 * (h % 2)
            gm_ps.wait(dve, l, h + 1)
            nc.vector.tensor_tensor(halves(qT[:, h, :]), halves(qT[:, h, :]), bank(b), ALU.subtract).then_inc(gc_sb.sem, 1)
            nc.vector.drain()
            gv_ps.wait(dve, l, h + 1)
            nc.vector.tensor_scalar(halves(mrs), bank(b + 2), LN_EPS, None, ALU.add).then_inc(ge.sem, 1)
            gr.wait(dve, l, h + 1)
            nc.vector.reciprocal(mrs, mrs)
            nc.vector.drain()
            nc.vector.tensor_tensor(qT[:, h, :], qT[:, h, :], mrs, ALU.mult)
            nc.vector.drain()
            nc.vector.scalar_tensor_tensor(qT[:, h, :], qT[:, h, :], pr["gn"][:, h:h + 1], sg[:, h, :], ALU.mult, ALU.mult).then_inc(gy_sb.sem, 1)
        for m in range(DK):
            wo_ps.wait(dve, l, m + 1)
            nc.vector.scalar_tensor_tensor(halves(res[:, m, :]), halves(hT[:, m, :]), ALPHA, bank(2 * (m % 4)), ALU.mult, ALU.add).then_inc(wo_sb.sem, 1)

    with nc.Block("layers") as block:
        @block.sync
        def _(sp):
            for n in range(RING, NL * LAYC):
                sz = CSIZE[n % LAYC]
                sp.wait_ge(used, W1N + WEN + n - RING + 1)
                sp.dma_start(slots[n % RING][:, 0:sz], A["wts"][W1N + WEN + n, :, 0:sz]).then_inc(arrived[n % RING], 16)
            for s in range(RING):
                sp.wait_ge(arrived[s], 16 * (base[s] + NL * LAYC // RING))

        @block.tensor
        def _(pe):
            ln_pe(pe, None, 0, lambda pe, k: None)
            with pe.Fori(0, NL) as l:
                ffn_pe(pe, l, 0)
                ln_pe(pe, l, 0, lambda pe, k: dn_sb.wait(pe, l, max(k + 1, 5)))
                par_in.wait(pe, l, 16)
                mix_pe(pe, l)
                ln_pe(pe, l, 1, lambda pe, k: wo_sb.wait(pe, l, max(k + 1, 5)))
                ffn_pe(pe, l, 1)
                ln_pe(pe, l, 2, lambda pe, k: dn_sb.wait(pe, l, DK + max(k + 1, 5)))

        @block.scalar
        def _(act):
            ln_act(act, None, 0, lnin[:, 0:DK], lnin[:, DK:])
            with act.Fori(0, NL) as l:
                nc.scalar.drain()
                act.dma_start(par, A["par"][bass.ds(l, 1), :, :].rearrange("a p n -> (a p) n")).then_inc(par_in.sem, 16)
                ffn_act(act, l, 0)
                par_in.wait(act, l, 16)
                for uu in range(3):
                    ln_act(act, l, uu, pr["ln_g"][:, uu * DK:(uu + 1) * DK], pr["ln_b"][:, uu * DK:(uu + 1) * DK])
                    if uu == 0:
                        mix_act(act, l)
                    elif uu == 1:
                        ffn_act(act, l, 1)

        @block.gpsimd
        def _(pool):
            with pool.Fori(0, NL) as l:
                mix_pool(pool, l)

        @block.vector
        def _(dve):
            ln_dve(dve, None, 0)
            with dve.Fori(0, NL) as l:
                ffn_dve(dve, l, 0)
                ln_dve(dve, l, 0)
                mix_dve(dve, l)
                ln_dve(dve, l, 1)
                ffn_dve(dve, l, 1)
                ln_dve(dve, l, 2)

    fo_ps, fo_a, fo_v, stored = sem("fo_ps"), sem("fo_a"), sem("fo_v"), sem("stored")
    ot = Map(arena, gT_at, gT_at + FT * L).take(TT, D)
    with nc.Block("store") as block:
        @block.tensor
        def _(pe):
            for g in range(2 * TT):
                t, half = divmod(g, 2)
                for i in range(4):
                    s = NMETA + t * P
                    last = nc.tensor.transpose(PS[:, g, i * P:(i + 1) * P], hT[:, half * 4 + i, s:s + P], C["ident"])
                last.then_inc(fo_ps, 1)

        @block.scalar
        def _(act):
            for t in range(TT):
                act.wait_ge(fo_ps, 2 * t + 1)
                nc.scalar.activation(ot[:, t, 0:512], PS[:, 2 * t, :], ACT.Copy).then_inc(fo_a, 1)

        @block.vector
        def _(dve):
            for t in range(TT):
                dve.wait_ge(fo_ps, 2 * t + 2)
                nc.vector.tensor_copy(ot[:, t, 512:], PS[:, 2 * t + 1, :]).then_inc(fo_v, 1)

        @block.sync
        def _(sp):
            for t in range(TT):
                sp.wait_ge(fo_a, t + 1)
                sp.wait_ge(fo_v, t + 1)
                sp.dma_start(E["out"][t * P:(t + 1) * P, :], ot[:, t, :]).then_inc(stored, 16)
            sp.wait_ge(stored, 16 * TT)



def cols(w, c0, n):
    return w[:, c0:c0 + n].reshape(-1, P, n).transpose(1, 0, 2)


def lay_out_rest(f, w):
    def tiles(m, c0, nt):
        return m[:, c0:c0 + nt * P].reshape(-1, P, nt, P).transpose(1, 2, 0, 3)
    for i in range(NE // 2):
        b = W1N + 2 * RING * i
        for j in range(2):
            for half in range(2):
                w[b + 4 * j + 2 * half] = cols(f["w_gate"][0, 2 * i + j], half * 512, 512).reshape(P, SLOT)
                w[b + 4 * j + 2 * half + 1] = cols(f["w_up"][0, 2 * i + j], half * 512, 512).reshape(P, SLOT)
                w[b + 8 + 2 * half + j] = cols(f["w_down"][0, 2 * i + j], half * 512, 512).reshape(P, SLOT)
    if PHASES < 6:
        return
    for l in range(NL):
        at = W1N + WEN + LAYC * l
        for kind, name in enumerate(("ffn1", "ffn2")):
            b = at + kind * (W13C + W2C + 10)
            m = np.zeros((D, 2, FT * P), np.float32)
            m[:, :, :DFF] = f[name + "_w13_2"][l].reshape(D, 2, DFF)
            t = m.reshape(DK, P, 2, W13C, 2, P).transpose(3, 1, 4, 2, 0, 5)
            w[b:b + W13C] = t.reshape(W13C, P, SLOT)
            m = np.zeros((FT * P, D), np.float32)
            m[:DFF] = f[name + "_w2_2"][l]
            w[b + W13C:b + W13C + W2C, :, :FT * P] = m.reshape(FT, P, DK, P).transpose(2, 1, 0, 3).reshape(DK, P, FT * P)
        b = at + W13C + W2C
        wi = f["w_in_2"][l]
        for j, (c0, nt) in enumerate([(0, 4), (512, 2), (768, 4), (1280, 4), (2304, 4)]):
            w[b + j, :, :nt * D] = tiles(wi, c0, nt).reshape(P, nt * D)
        w[b + 5] = cols(wi, 1792, 512).reshape(P, SLOT)
        for j in range(4):
            w[b + 6 + j, :, :2 * D] = tiles(f["w_out_2"][l], j * 256, 2).reshape(P, 2 * D)


def lay_out_second(f, a):
    a["tab2"] = np.concatenate(list(table2().values()), 1)
    feat = lambda v: v.reshape(-1, P).T
    a["ln_in"] = np.concatenate([feat(f["ln_in_g_2"]), feat(f["ln_in_b_2"])], 1)
    a["meta"] = f["meta_2"].reshape(NMETA, DK, P).transpose(2, 1, 0).reshape(P, DK * NMETA)
    rows = []
    for l in range(NL):
        pool = np.zeros((2, P, P), np.float32)
        for g in range(4):
            h = 64 * (g % 2)
            pool[g // 2, h:h + 64, h:h + 64] = f["pool_w_2"][l, g]
        rows.append(np.concatenate([
            feat(f["ln_g_2"][l]), feat(f["ln_b_2"][l]), feat(f["pool_scale_2"][l]), feat(f["conv_db_2"][l]),
            feat(f["conv_ln_g_2"][l]), feat(f["conv_ln_b_2"][l]), feat(f["ret_gn_g_2"][l]),
            f["conv_dw_2"][l].reshape(CW, 2, P).transpose(2, 1, 0).reshape(P, 2 * CW),
            pool.transpose(1, 0, 2).reshape(P, 2 * P), cols(f["conv_pw_2"][l], 0, 256).reshape(P, 512)], 1))
    a["par"] = np.stack(rows)


def lay_out(I):
    f = {k: np.asarray(v) for k, v in I.items()}
    w = np.zeros((W1N + WEN + NL * LAYC, P, SLOT), np.float32)
    for j in range(MODC):
        w[j] = cols(f["w_mod"][0], 512 * j, 512).reshape(P, SLOT)
    na = 4 * 512 + 16
    for j, c0 in enumerate([na, na + 512, na + 1024, 1536, 0, 512, 1024]):
        w[MODC + j] = cols(f["w_in"][0], c0, 512).reshape(P, SLOT)
    for j in range(OUTC):
        w[MODC + INC + j] = cols(f["w_out"][0], 512 * j, 512).reshape(P, SLOT)
    if PHASES >= 5:
        lay_out_rest(f, w)
    a = {"wts": w, "tab1": np.concatenate(list(table1().values()), 1)}
    a["cvec"] = np.concatenate([f["c"].reshape(DK, P).T, f["c_ctx"].reshape(DK, P).T], 1)
    for k in ("b_mod", "norm_mix", "norm_ffn", "gdn_norm", "final_norm"):
        a[k] = f[k].reshape(-1)
    a["x"], a["ctx"] = f["x"][0], f["ctx"][0]
    c = np.arange(GRID)
    cs = np.clip(c - NCOL // 2, 0, GRID - NCOL)
    inside = (c[None, :] >= cs[:, None]) & (c[None, :] < cs[:, None] + NCOL)
    idx = np.clip(c[None, :] - c[:, None], -(NCOL - 1), NCOL - 1) + NCOL - 1
    toe = np.where(inside, f["na_rpb"][0][:, :, idx], np.float32(-1e30))
    nb = np.full((HN, 2, GRID, 16, GRID), -1e30, np.float32)
    nb[:, 0, :, 0:15] = toe.transpose(0, 2, 1, 3)
    nb[:, 1, :, 1:16] = toe.transpose(0, 2, 1, 3)
    a["na_bias"] = nb.reshape(HN, P, 16 * GRID)
    a["w_ab"] = np.ascontiguousarray(cols(f["w_in"][0], 2048, 16)).reshape(P, DK * 16)
    a["conv"] = np.ascontiguousarray(f["conv_qkv"][0].reshape(CONV, 12, P).transpose(2, 1, 0)).reshape(P, 12 * CONV)
    a["a_log"], a["dt_bias"] = f["a_log"].reshape(-1), f["dt_bias"].reshape(-1)
    a["w_router"] = np.ascontiguousarray(cols(f["w_router"][0], 0, NE)).reshape(P, DK * NE)
    if PHASES >= 6:
        lay_out_second(f, a)
    return {k: np.ascontiguousarray(v, np.float32) for k, v in a.items()}


def kernel(**inputs):
    import concourse.bacc as bacc
    from concourse.bass_utils import run_bass_kernel_spmd as run

    nc = bacc.Bacc("TRN2", target_bir_lowering=False, num_devices=1)
    arrays = lay_out(inputs)
    aps = {k: nc.dram_tensor(k + "_dram", v.shape, F32, kind="ExternalInput").ap() for k, v in arrays.items()}
    out = nc.dram_tensor("out_dram", (T, D), F32, kind="ExternalOutput").ap()
    build(nc, aps, out)
    r = run(nc, [{k + "_dram": v for k, v in arrays.items()}], core_ids=[0])
    return r.results[0]["out_dram"].reshape(1, T, D)
```
